# Optimizing a Trainium2 kernel written in Bass

```python
import functools
import jax
import jax.numpy as jnp
from jax import lax
import numpy as np

D_MODEL = 1024
BATCH = 1
SEQ = 1024
DEPTH = 1
DEC_BATCH = 8
DEC_SEQ = 8
PAST_LEN = 8192
PAGE_SIZE = 128

N_Q_HEADS = 8
N_KV_HEADS = 2
HEAD_DIM = 64
GQA_GROUP = N_Q_HEADS // N_KV_HEADS
ATT_WIDTH = N_Q_HEADS * HEAD_DIM
KV_WIDTH = N_KV_HEADS * HEAD_DIM
WINDOW = 128
ROPE_THETA = 500000.0
ROT_DIM = HEAD_DIM // 4
POOL_WINDOWS = (2, 4, 8, 16)
POOL_GROUPS = 4
POOL_WIDTH = D_MODEL - ATT_WIDTH
POOL_GROUP_DIM = POOL_WIDTH // POOL_GROUPS
POOL_STATE = 15
MIX_WIDTH = ATT_WIDTH + POOL_WIDTH
IN_WIDTH = ATT_WIDTH + 2 * KV_WIDTH + POOL_WIDTH
N_EXPERTS = 64
TOP_K = 8
N_EXPERT_GROUPS = 8
TOPK_GROUPS = 4
D_EXPERT = 256
D_SHARED = 256
ROUTED_SCALE = 2.5
EXPERT_BLOCK = 128
PLE_DIM = 256
EPS = 1e-6

kernel_name = 'hymba_swa_sink_pool_moe_ple_step'

def rmsnorm(x, g):
    xf = x.astype(jnp.float32)
    y = xf * lax.rsqrt(jnp.mean(xf * xf, axis=-1, keepdims=True) + EPS)
    return (y * g.astype(jnp.float32)).astype(x.dtype)

def swiglu(x, w_gate, w_up, w_down):
    return (jax.nn.silu(x @ w_gate) * (x @ w_up)) @ w_down

def partial_rope(x, pos):
    half = ROT_DIM // 2
    inv = ROPE_THETA ** (-jnp.arange(half, dtype=jnp.float32) * 2.0 / ROT_DIM)
    ang = pos.astype(jnp.float32)[:, None] * inv[None, :]
    cos = jnp.cos(ang)[:, None, :]
    sin = jnp.sin(ang)[:, None, :]
    xr = x[..., :ROT_DIM].astype(jnp.float32)
    x1, x2 = xr[..., :half], xr[..., half:]
    rot = jnp.concatenate([x1 * cos - x2 * sin, x2 * cos + x1 * sin], axis=-1)
    return jnp.concatenate([rot.astype(x.dtype), x[..., ROT_DIM:]], axis=-1)

def sink_attention(q, k, v, mask, sinks):
    s = jnp.einsum('...qhgd,...khd->...hgqk', q.astype(jnp.float32), k.astype(jnp.float32)) * (HEAD_DIM ** -0.5)
    s = jnp.where(mask[..., None, None, :, :], s, -jnp.inf)
    sink = sinks.astype(jnp.float32).reshape(N_KV_HEADS, GQA_GROUP)[:, :, None, None]
    m = jnp.maximum(jnp.max(s, axis=-1, keepdims=True), sink)
    e = jnp.exp(s - m)
    p = e / (jnp.sum(e, axis=-1, keepdims=True) + jnp.exp(sink - m))
    o = jnp.einsum('...hgqk,...khd->...qhgd', p, v.astype(jnp.float32))
    return o.astype(q.dtype)

def attend_prompt(q, k, v, sinks):
    B, S = q.shape[:2]
    nb = S // WINDOW
    qb = q.reshape(B, nb, WINDOW, N_KV_HEADS, GQA_GROUP, HEAD_DIM)
    kb = k.reshape(B, nb, WINDOW, N_KV_HEADS, HEAD_DIM)
    vb = v.reshape(B, nb, WINDOW, N_KV_HEADS, HEAD_DIM)
    kk = jnp.concatenate([jnp.concatenate([jnp.zeros_like(kb[:, :1]), kb[:, :-1]], axis=1), kb], axis=2)
    vv = jnp.concatenate([jnp.concatenate([jnp.zeros_like(vb[:, :1]), vb[:, :-1]], axis=1), vb], axis=2)
    qpos = jnp.arange(S, dtype=jnp.int32).reshape(nb, WINDOW)
    kpos = qpos[:, :1] - WINDOW + jnp.arange(2 * WINDOW, dtype=jnp.int32)[None, :]
    diff = qpos[:, :, None] - kpos[:, None, :]
    mask = (diff >= 0) & (diff <= WINDOW) & (kpos[:, None, :] >= 0)
    o = sink_attention(qb, kk, vv, mask, sinks)
    return o.reshape(B, S, ATT_WIDTH), k[:, -WINDOW:], v[:, -WINDOW:]

def attend_sample(q, k, v, sinks, k_cache, v_cache, q_pos):
    B, S = q.shape[:2]
    C = k_cache.shape[1]
    kk = jnp.concatenate([k_cache.astype(k.dtype), k], axis=1)
    vv = jnp.concatenate([v_cache.astype(v.dtype), v], axis=1)
    kpos = jnp.concatenate([q_pos[0] - C + jnp.arange(C, dtype=jnp.int32), q_pos])
    diff = q_pos[:, None] - kpos[None, :]
    mask = (diff >= 0) & (diff <= WINDOW) & (kpos[None, :] >= 0)
    o = sink_attention(q, kk, vv, mask, sinks)
    return o.reshape(B, S, ATT_WIDTH), kk[:, -C:], vv[:, -C:]

def pool_mix(u_ext, q_pos, w_pool, pool_scale):
    B, n = u_ext.shape[0], q_pos.shape[0]
    f = u_ext.astype(jnp.float32)
    cs = jnp.concatenate([jnp.zeros_like(f[:, :1]), jnp.cumsum(f, axis=1)], axis=1)
    hi = cs[:, POOL_STATE + 1:]
    parts = []
    for g, w in enumerate(POOL_WINDOWS):
        c0, c1 = g * POOL_GROUP_DIM, (g + 1) * POOL_GROUP_DIM
        lo = cs[:, POOL_STATE + 1 - w:POOL_STATE + 1 - w + n, c0:c1]
        count = jnp.minimum(q_pos + 1, w).astype(jnp.float32)[:, None]
        parts.append((hi[..., c0:c1] - lo) / count)
    d = (jnp.concatenate(parts, axis=-1) - f[:, POOL_STATE:]).reshape(B, n, POOL_GROUPS, POOL_GROUP_DIM)
    y = jnp.einsum('bsgc,gcd->bsgd', d, w_pool.astype(jnp.float32)).reshape(B, n, POOL_WIDTH)
    return (y * pool_scale.astype(jnp.float32)).astype(u_ext.dtype)

def routed_experts(xf, idx, wts, w_gate, w_up, w_down):
    T, D = xf.shape
    A = T * TOP_K
    n_blocks = -(-A // EXPERT_BLOCK) + N_EXPERTS
    flat_e = idx.reshape(A).astype(jnp.int32)
    flat_tok = jnp.repeat(jnp.arange(T, dtype=jnp.int32), TOP_K)
    flat_w = wts.reshape(A)
    order = jnp.argsort(flat_e)
    e_sorted = flat_e[order]
    counts = jnp.bincount(flat_e, length=N_EXPERTS).astype(jnp.int32)
    padded = (counts + EXPERT_BLOCK - 1) // EXPERT_BLOCK * EXPERT_BLOCK
    pad_end = jnp.cumsum(padded)
    pad_start = pad_end - padded
    start = jnp.cumsum(counts) - counts
    dest = pad_start[e_sorted] + jnp.arange(A, dtype=jnp.int32) - start[e_sorted]
    slots = n_blocks * EXPERT_BLOCK
    slot_tok = jnp.full((slots,), T, jnp.int32).at[dest].set(flat_tok[order])
    slot_w = jnp.zeros((slots,), xf.dtype).at[dest].set(flat_w[order])
    block_start = jnp.arange(n_blocks, dtype=jnp.int32) * EXPERT_BLOCK
    block_e = jnp.minimum(jnp.searchsorted(pad_end, block_start, side='right'), N_EXPERTS - 1)
    x_pad = jnp.concatenate([xf, jnp.zeros((1, D), xf.dtype)], axis=0)

    def body(acc, blk):
        tok, w, e = blk
        xb = x_pad[tok]
        yb = swiglu(xb, w_gate[e], w_up[e], w_down[e]) * w[:, None]
        return acc.at[tok].add(yb), None

    acc, _ = lax.scan(body, jnp.zeros((T + 1, D), xf.dtype),
                      (slot_tok.reshape(n_blocks, EXPERT_BLOCK), slot_w.reshape(n_blocks, EXPERT_BLOCK), block_e))
    return acc[:T]

def moe_ffn(x, w_router, router_bias, w_exp_gate, w_exp_up, w_exp_down, w_sh_gate, w_sh_up, w_sh_down):
    B, S, D = x.shape
    xf = x.reshape(B * S, D)
    T = xf.shape[0]
    scores = jax.nn.sigmoid(xf.astype(jnp.float32) @ w_router.astype(jnp.float32))
    biased = scores + router_bias.astype(jnp.float32)
    grp_score = jnp.sum(lax.top_k(biased.reshape(T, N_EXPERT_GROUPS, -1), 2)[0], axis=-1)
    _, top_g = lax.top_k(grp_score, TOPK_GROUPS)
    gmask = jnp.any(top_g[..., None] == jnp.arange(N_EXPERT_GROUPS)[None, None, :], axis=1)
    emask = jnp.repeat(gmask, N_EXPERTS // N_EXPERT_GROUPS, axis=1)
    _, idx = lax.top_k(jnp.where(emask, biased, -jnp.inf), TOP_K)
    sel = jnp.take_along_axis(scores, idx, axis=1)
    wts = (sel / jnp.sum(sel, axis=-1, keepdims=True) * ROUTED_SCALE).astype(xf.dtype)
    routed = routed_experts(xf, idx, wts, w_exp_gate, w_exp_up, w_exp_down)
    shared = swiglu(xf, w_sh_gate, w_sh_up, w_sh_down)
    return (routed + shared).reshape(B, S, D)

def decoder_layer(h, p_i, q_pos, attend, pool_prefix, g_mix, w_in, w_pool, pool_scale, g_att_out, g_pool_out,
                  w_out, g_ffn, w_router, router_bias, w_exp_gate, w_exp_up, w_exp_down, w_sh_gate, w_sh_up,
                  w_sh_down, g_ple, w_ple_gate, w_ple_proj):
    B, S, _ = h.shape
    z = rmsnorm(h, g_mix) @ w_in
    q = z[..., :ATT_WIDTH].reshape(B, S, N_Q_HEADS, HEAD_DIM)
    k = z[..., ATT_WIDTH:ATT_WIDTH + KV_WIDTH].reshape(B, S, N_KV_HEADS, HEAD_DIM)
    v = z[..., ATT_WIDTH + KV_WIDTH:ATT_WIDTH + 2 * KV_WIDTH].reshape(B, S, N_KV_HEADS, HEAD_DIM)
    u = z[..., ATT_WIDTH + 2 * KV_WIDTH:]
    q = partial_rope(q, q_pos).reshape(B, S, N_KV_HEADS, GQA_GROUP, HEAD_DIM)
    k = partial_rope(k, q_pos)
    o_att, k_state, v_state = attend(q, k, v)
    u_ext = jnp.concatenate([pool_prefix.astype(u.dtype), u], axis=1)
    o_pool = pool_mix(u_ext, q_pos, w_pool, pool_scale)
    mixed = jnp.concatenate([rmsnorm(o_att, g_att_out), rmsnorm(o_pool, g_pool_out)], axis=-1)
    h = h + mixed @ w_out
    h = h + moe_ffn(rmsnorm(h, g_ffn), w_router, router_bias, w_exp_gate, w_exp_up, w_exp_down,
                    w_sh_gate, w_sh_up, w_sh_down)
    h = h + (p_i.astype(h.dtype) @ w_ple_proj) * jax.nn.sigmoid(rmsnorm(h, g_ple) @ w_ple_gate)
    return h, k_state, v_state, u_ext[:, -POOL_STATE:]

def setup_inputs(seed: int = 0) -> dict:
    key = jax.random.key(seed)
    ks = jax.random.split(key, 32)

    def nrm(k, shape, scale):
        return jax.random.normal(k, shape, jnp.float32) * scale

    win = min(WINDOW, PAST_LEN)
    L = DEPTH
    return {
        'x_prompt': nrm(ks[0], (BATCH, SEQ, D_MODEL), 1.0),
        'x_sample': nrm(ks[1], (DEC_BATCH, DEC_SEQ, D_MODEL), 1.0),
        'cache_k': nrm(ks[2], (L, DEC_BATCH, win, N_KV_HEADS, HEAD_DIM), 1.0),
        'cache_v': nrm(ks[3], (L, DEC_BATCH, win, N_KV_HEADS, HEAD_DIM), 1.0),
        'state_pool': nrm(ks[4], (L, DEC_BATCH, POOL_STATE, POOL_WIDTH), 1.0),
        'p_prompt': nrm(ks[5], (L, BATCH, SEQ, PLE_DIM), 1.0),
        'p_sample': nrm(ks[6], (L, DEC_BATCH, DEC_SEQ, PLE_DIM), 1.0),
        'g_mix': 1.0 + nrm(ks[7], (L, D_MODEL), 0.02),
        'w_in': nrm(ks[8], (L, D_MODEL, IN_WIDTH), D_MODEL ** -0.5),
        'attn_sinks': nrm(ks[9], (L, N_Q_HEADS), 1.0),
        'w_pool': nrm(ks[10], (L, POOL_GROUPS, POOL_GROUP_DIM, POOL_GROUP_DIM), POOL_GROUP_DIM ** -0.5),
        'pool_scale': 1.0 + nrm(ks[11], (L, POOL_WIDTH), 0.1),
        'g_att_out': 1.0 + nrm(ks[12], (L, ATT_WIDTH), 0.02),
        'g_pool_out': 1.0 + nrm(ks[13], (L, POOL_WIDTH), 0.02),
        'w_out': nrm(ks[14], (L, MIX_WIDTH, D_MODEL), MIX_WIDTH ** -0.5),
        'g_ffn': 1.0 + nrm(ks[15], (L, D_MODEL), 0.02),
        'w_router': nrm(ks[16], (L, D_MODEL, N_EXPERTS), D_MODEL ** -0.5),
        'router_bias': nrm(ks[17], (L, N_EXPERTS), 0.01),
        'w_exp_gate': nrm(ks[18], (L, N_EXPERTS, D_MODEL, D_EXPERT), D_MODEL ** -0.5),
        'w_exp_up': nrm(ks[19], (L, N_EXPERTS, D_MODEL, D_EXPERT), D_MODEL ** -0.5),
        'w_exp_down': nrm(ks[20], (L, N_EXPERTS, D_EXPERT, D_MODEL), D_EXPERT ** -0.5),
        'w_sh_gate': nrm(ks[21], (L, D_MODEL, D_SHARED), D_MODEL ** -0.5),
        'w_sh_up': nrm(ks[22], (L, D_MODEL, D_SHARED), D_MODEL ** -0.5),
        'w_sh_down': nrm(ks[23], (L, D_SHARED, D_MODEL), D_SHARED ** -0.5),
        'g_ple': 1.0 + nrm(ks[24], (L, D_MODEL), 0.02),
        'w_ple_gate': nrm(ks[25], (L, D_MODEL, D_MODEL), D_MODEL ** -0.5),
        'w_ple_proj': nrm(ks[26], (L, PLE_DIM, D_MODEL), PLE_DIM ** -0.5),
        'g_final': 1.0 + nrm(ks[27], (D_MODEL,), 0.02),
    }

def reference(x_prompt, x_sample, cache_k, cache_v, state_pool, p_prompt, p_sample, g_mix, w_in, attn_sinks,
              w_pool, pool_scale, g_att_out, g_pool_out, w_out, g_ffn, w_router, router_bias, w_exp_gate,
              w_exp_up, w_exp_down, w_sh_gate, w_sh_up, w_sh_down, g_ple, w_ple_gate, w_ple_proj, g_final):
    hp, hs = x_prompt, x_sample
    kp, vp, pp, ksl, vsl, psl = [], [], [], [], [], []
    pos_p = jnp.arange(x_prompt.shape[1], dtype=jnp.int32)
    pos_s = PAST_LEN + jnp.arange(x_sample.shape[1], dtype=jnp.int32)
    for i in range(DEPTH):
        lw = (g_mix[i], w_in[i], w_pool[i], pool_scale[i], g_att_out[i], g_pool_out[i], w_out[i], g_ffn[i],
              w_router[i], router_bias[i], w_exp_gate[i], w_exp_up[i], w_exp_down[i], w_sh_gate[i], w_sh_up[i],
              w_sh_down[i], g_ple[i], w_ple_gate[i], w_ple_proj[i])
        att_p = functools.partial(attend_prompt, sinks=attn_sinks[i])
        prefix_p = jnp.zeros((hp.shape[0], POOL_STATE, POOL_WIDTH), hp.dtype)
        hp, k1, v1, s1 = decoder_layer(hp, p_prompt[i], pos_p, att_p, prefix_p, *lw)
        att_s = functools.partial(attend_sample, sinks=attn_sinks[i], k_cache=cache_k[i], v_cache=cache_v[i],
                                  q_pos=pos_s)
        hs, k2, v2, s2 = decoder_layer(hs, p_sample[i], pos_s, att_s, state_pool[i], *lw)
        kp.append(k1)
        vp.append(v1)
        pp.append(s1)
        ksl.append(k2)
        vsl.append(v2)
        psl.append(s2)
    y_prompt = rmsnorm(hp, g_final)
    y_sample = rmsnorm(hs, g_final)
    return (y_prompt, y_sample, jnp.stack(kp), jnp.stack(vp), jnp.stack(pp), jnp.stack(ksl), jnp.stack(vsl), jnp.stack(psl))


_drawn_inputs = setup_inputs


def setup_inputs(seed=0):
    import zlib

    import numpy as np

    out = dict(_drawn_inputs(seed))
    spreads = {}
    factors = {'g_ple': 154.406, 'g_final': 30.096}
    for name, (base, spread) in spreads.items():
        noise = np.random.default_rng([zlib.crc32(name.encode()), seed]).standard_normal(out[name].shape)
        drawn = base * np.exp(spread * noise) if base else spread * noise
        out[name] = jnp.asarray(drawn.astype(out[name].dtype))
    for name, factor in factors.items():
        out[name] = (out[name] * factor).astype(out[name].dtype)
    return out
```

```python
from contextlib import ExitStack

import numpy as np
import concourse.bass as bass
from concourse import mybir

F32 = mybir.dt.float32
F32R = mybir.dt.float32r
BF16 = mybir.dt.bfloat16
I32 = mybir.dt.int32
U32 = mybir.dt.uint32
ALU = mybir.AluOpType
ACT = mybir.ActivationFunctionType
AX = mybir.AxisListType

P = 128
D = 1024
SEQ = 1024
PROMPT_TILES = SEQ // P
SEQS = 8
STEPS = 8
NS = SEQS * STEPS
TILES = PROMPT_TILES + 1
SAMPLE = PROMPT_TILES
LAST_PROMPT = PROMPT_TILES - 1
PAST = 8192
HEADS, KV_HEADS, HD = 8, 2, 64
GROUP = HEADS // KV_HEADS
ATT = HEADS * HD
KV = KV_HEADS * HD
POOL = D - ATT
IN_W = ATT + 2 * KV + POOL
K0, V0, U0 = ATT, ATT + KV, ATT + 2 * KV
WINDOW = 128
HALF = HD // 8
THETA = 500000.0
POOL_WINDOWS = (2, 4, 8, 16)
PG = len(POOL_WINDOWS)
PREFIX = 15
KC = D // P
E = 64
EG = 8
TOP = 8
TOP_GROUPS = 4
FE = 256
FC = FE // P
ROUTED_SCALE = 2.5
PLE = 256
EPS = 1e-6
SCALE = HD ** -0.5
NEG = -1e30
CAP = 212
ROUNDS = -(-(SEQ + NS) // CAP)
BLK = (P, CAP - P)
OVER_ROW = E * CAP
SPARE_ROW = OVER_ROW + (SEQ + NS) * TOP
Y_ROWS = SPARE_ROW + CAP


def after(eng, sem, value):
    if not (isinstance(value, int) and value <= 0):
        eng.wait_ge(sem, value)


def pool_after(pool, passed, sem, value):
    after(pool, sem, value)
    pool.sem_inc(passed, 1)


class Chain:

    def __init__(self, eng, sem):
        self.eng, self.sem, self.n = eng, sem, 0

    def did(self, ins):
        ins.then_inc(self.sem, 1)
        self.n += 1

    def wait(self):
        self.eng.wait_ge(self.sem, self.n)

    def clear(self):
        self.wait()
        self.eng.sem_clear(self.sem)
        self.n = 0


def rstd(own, pool, dst, src, width, half, ready):
    own.did(pool.tensor_scalar(dst, src, 1.0 / width, EPS, ALU.mult, ALU.add))
    own.wait()
    pool.tensor_tensor(dst, dst, half, ALU.pow).then_inc(ready, 1)


def build(nc, a, o, c):
    rows_dram = nc.dram_tensor("rows_dram", (TILES * P, D), F32, kind="Internal").ap()
    y_dram = nc.dram_tensor("y_dram", (Y_ROWS, D), F32, kind="Internal").ap()
    o_dram = nc.dram_tensor("o_dram", (4, P, HD), F32, kind="Internal").ap()

    with ExitStack() as ctx:
        def sb(name, shape, dt=F32):
            return ctx.enter_context(nc.sbuf_tensor(name, shape, dt))
        keep = dict(
            resid=sb("resid", [P, TILES, D]),
            ident=sb("ident", [P, P]),
            raw_g=sb("raw_g", [P, KC, FE]), raw_u=sb("raw_u", [P, KC, FE]), raw_d=sb("raw_d", [P, FC, D]),
            place=sb("place", [P, E + 3, TILES]),
            w8=sb("w8", [P, TILES, TOP]),
            slots=sb("slots", [P, TILES * TOP], I32),
            rounds=sb("rounds", [1, 1], I32),
            y_row=sb("y_row", [1, ROUNDS * E], I32),
            **{n: ctx.enter_context(nc.semaphore(n)) for n in ("g_ld", "u_ld", "d_ld", "passed")},
        )
        mixer(nc, a, o, c, keep, o_dram)
        router(nc, a, c, keep, rows_dram, y_dram)
        experts(nc, a, c, keep, rows_dram, y_dram)
        output(nc, a, o, keep, y_dram)



def mixer(nc, a, o, c, keep, o_dram):
    resid, ident = keep["resid"], keep["ident"]
    with ExitStack() as ctx:
        def sb(name, shape, dt=F32):
            return ctx.enter_context(nc.sbuf_tensor(name, shape, dt))

        def sem(name):
            return ctx.enter_context(nc.semaphore(name))

        w_in = sb("w_in", [P, KC, IN_W])
        w_out = sb("w_out", [P, KC, D])
        w_pool = sb("w_pool", [P, PG, P])
        g_mix = sb("g_mix", [P, D])
        g_mid = sb("g_mid", [P, D])
        p_scale = sb("p_scale", [P, POOL])
        sink = sb("sink", [P, HEADS])
        sink_s = sb("sink_s", [P, KV_HEADS])
        pick = sb("pick", [P, KV_HEADS, HEADS])
        picked = sb("picked", [P, KV_HEADS, HEADS])
        rope = sb("rope", [P, TILES, 2, HALF])
        amask = sb("amask", [P, 2, 2 * P])
        smask = sb("smask", [P, 2, P + NS])
        pmat = sb("pmat", [P, 3, PG, P])
        row = sb("row", [P, D])
        colT = sb("colT", [P, KC, P])
        colM = sb("colM", [P, KC, P])
        z = sb("z", [P, IN_W])
        rt = sb("rt", [P, 4, HEADS + KV_HEADS, HALF])
        qT = sb("qT", [P, GROUP, P])
        kT = sb("kT", [P, 2 * P])
        v_prev = sb("v_prev", [P, KV])
        u_prev = sb("u_prev", [P, POOL])
        prob = sb("prob", [P, HEADS, 2 * P])
        probT = sb("probT", [P, HEADS, 2, P])
        dT = sb("dT", [P, PG, P])
        mix = sb("mix", [P, D])
        junk = sb("junk", [P, D], BF16)
        st = sb("st", [P, 8])
        half = sb("half", [P, 2])
        mx = sb("mx", [P, HEADS])
        m8 = sb("m8", [P, 3, HEADS])
        den = sb("den", [P, HEADS])
        rden = sb("rden", [P, HEADS])
        late = keep["raw_d"][:].rearrange("p f d -> p (f d)")
        vc = late[:, 0:SEQS * KV].rearrange("p (b k) -> p b k", b=SEQS)
        ustate = late[0:SEQS * PREFIX, 1024:1024 + POOL]
        pmat_s = late[:, 1536:2048].rearrange("p (a g q) -> p a g q", a=2, g=PG)
        o_s = keep["place"][:].rearrange("p e t -> p (e t)")[:, 0:4 * HD].rearrange("p (c d) -> p c d", c=4)
        kc = probT[:].rearrange("p h b q -> p (h b q)")[:, 0:SEQS * KV].rearrange("p (b k) -> p b k", b=SEQS)
        kcT = probT[:].rearrange("p h b q -> p (h b q)")[:, SEQS * KV:2 * SEQS * KV].rearrange(
            "p (b k) -> p b k", b=SEQS)
        prob_s = prob[:].rearrange("p h k -> p (h k)")[:, 0:4 * (P + NS)].rearrange("p (c k) -> p c k", c=4)
        ptc = prob[:].rearrange("p h k -> p (h k)")[:, 1024:1024 + 4 * P].rearrange("p (c k) -> p c k", c=4)
        ptn = prob[:].rearrange("p h k -> p (h k)")[:, 1536:1536 + 4 * P].rearrange("p (c k) -> p c k", c=4)

        X = [ctx.enter_context(nc.psum_tensor(f"X{i}", [P, 512], F32)) for i in range(2)]
        Z = [ctx.enter_context(nc.psum_tensor(f"Z{i}", [P, 512], F32)) for i in range(2)]
        S = [ctx.enter_context(nc.psum_tensor(f"S{i}", [P, 512], F32)) for i in range(4)]

        x0_ld, g_mix_ld, x_ld, wout_ld, c_ld, late_ld, cache_ld = (sem(n) for n in (
            "x0_ld", "g_mix_ld", "x_ld", "wout_ld", "c_ld", "late_ld", "cache_ld"))
        win_ld = [sem(f"win_ld{i}") for i in range(3)]
        ident_set, zeroed, sumsq, xs_ready, x_tr, x_ev, z_done, zq_ev, zk_ev = (sem(n) for n in (
            "ident_set", "zeroed", "sumsq", "xs_ready", "x_tr", "x_ev", "z_done", "zq_ev", "zk_ev"))
        roped, d_done, dT_ev, qk_tr, qk_ev, s_done, y_done, m_ready, p_ready = (sem(n) for n in (
            "roped", "d_done", "dT_ev", "qk_tr", "qk_ev", "s_done", "y_done", "m_ready", "p_ready"))
        pt_tr, pt_dve, pt_act, o_done, prev_copied, mix_raw, mix_sq, mixed, m_tr, m_ev = (
            sem(n) for n in ("pt_tr", "pt_dve", "pt_act", "o_done", "prev_copied", "mix_raw", "mix_sq", "mixed",
                             "m_tr", "m_ev"))
        proj_done, added = ([sem(f"{n}{half}") for half in range(2)] for n in ("proj_done", "added"))
        kv_out, kc_tr, kc_ev, pts_ev, os_ready, o_st, o_back, copied = (sem(n) for n in (
            "kv_out", "kc_tr", "kc_ev", "pts_ev", "os_ready", "o_st", "o_back", "copied"))
        dve_own, pool_own, x_rstd, m_rstd = sem("dve_own_mixer"), sem("pool_own_mixer"), sem("x_rstd"), sem("m_rstd")

        NCONST = 8
        Z_IN = ((S[1], 0, 512), (S[2], 512, 1024), (S[3], 1024, IN_W))

        block = ctx.enter_context(nc.Block())

        @block.sync
        def _(sp):
            sp.dma_start(resid[:, 0, :], a["x_prompt"][0, 0:P, :]).then_inc(x0_ld, 16)
            sp.dma_start(g_mix[:], a["g_mix"][0:1, :].broadcast_to([P, D])).then_inc(g_mix_ld, 16)
            for i, (_, n0, n1) in enumerate(Z_IN):
                sp.dma_start(w_in[:, :, n0:n1], a["w_in"][0].rearrange("(p k) n -> p k n", k=KC)[:, :, n0:n1]).then_inc(
                    win_ld[i], 16)
                if i == 0:
                    sp.dma_start(rope[:], c["rope"]).then_inc(c_ld, 16)
            sp.dma_start(amask[:], c["amask"]).then_inc(c_ld, 16)
            sp.dma_start(pmat[:], c["pmat"]).then_inc(c_ld, 16)
            sp.dma_start(w_pool[:], a["w_pool"][0].rearrange("g c d -> c g d")).then_inc(c_ld, 16)
            sp.dma_start(p_scale[:], a["pool_scale"][0:1, :].broadcast_to([P, POOL])).then_inc(c_ld, 16)
            sp.dma_start(sink[:], a["attn_sinks"][0:1, :].broadcast_to([P, HEADS])).then_inc(c_ld, 16)
            sp.dma_start(resid[:, 1:PROMPT_TILES, :],
                         a["x_prompt"][0, P:SEQ, :].rearrange("(t p) d -> p t d", p=P)).then_inc(x_ld, 16)
            sp.dma_start(resid[0:NS, SAMPLE, :], a["x_sample"].rearrange("b s d -> (b s) d")).then_inc(x_ld, 16)
            sp.dma_start(g_mid[:, 0:ATT], a["g_att_out"][0:1, :].broadcast_to([P, ATT])).then_inc(c_ld, 16)
            sp.dma_start(g_mid[:, ATT:D], a["g_pool_out"][0:1, :].broadcast_to([P, POOL])).then_inc(c_ld, 16)
            sp.dma_start(w_out[:], a["w_out"][0].rearrange("(p k) n -> p k n", k=KC)).then_inc(wout_ld, 16)
            sp.dma_start(smask[:], c["smask"]).then_inc(late_ld, 16)
            sp.dma_start(pmat_s, c["pmat_s"]).then_inc(late_ld, 16)
            sp.dma_start(ustate, a["state_pool"][0].rearrange("b r u -> (b r) u")).then_inc(late_ld, 16)
            sp.dma_start(pick[:], c["pick"]).then_inc(late_ld, 16)
            sp.dma_start(vc, a["cache_v"][0].rearrange("b p g d -> p b (g d)")).then_inc(cache_ld, 16)
            for src, dst in ((a["cache_k"], o["k_sample"]), (a["cache_v"], o["v_sample"])):
                sp.dma_start(dst[0, :, 0:WINDOW - STEPS], src[0, :, STEPS:WINDOW]).then_inc(copied, 16)
            sp.dma_start(o["pool_sample"][0, :, 0:PREFIX - STEPS],
                         a["state_pool"][0, :, STEPS:PREFIX]).then_inc(copied, 16)
            sp.dma_start(keep["raw_g"][:], a["w_exp_gate"][0, 0].rearrange("(p k) f -> p k f", k=KC)).then_inc(
                keep["g_ld"], 16)
            sp.dma_start(keep["raw_u"][:], a["w_exp_up"][0, 0].rearrange("(p k) f -> p k f", k=KC)).then_inc(
                keep["u_ld"], 16)
            sp.wait_ge(roped, PROMPT_TILES)
            sp.wait_ge(zk_ev, 2 * PROMPT_TILES)
            sp.dma_start(o["k_prompt"][0, 0].rearrange("w g d -> w (g d)"), z[:, K0:V0]).then_inc(kv_out, 16)
            sp.dma_start(o["v_prompt"][0, 0].rearrange("w g d -> w (g d)"), z[:, V0:U0]).then_inc(kv_out, 16)
            sp.dma_start(o["pool_prompt"][0, 0], z[P - PREFIX:P, U0:IN_W]).then_inc(kv_out, 16)
            sp.wait_ge(o_done, PROMPT_TILES)
            sp.dma_start(kc, a["cache_k"][0].rearrange("b p g d -> p b (g d)")).then_inc(cache_ld, 16)
            sp.wait_ge(roped, TILES)
            sp.wait_ge(zk_ev, 2 * TILES)
            for b in range(SEQS):
                r = slice(b * STEPS, (b + 1) * STEPS)
                new = slice(WINDOW - STEPS, WINDOW)
                sp.dma_start(o["k_sample"][0, b, new].rearrange("w g d -> w (g d)"), z[r, K0:V0]).then_inc(copied, 16)
                sp.dma_start(o["v_sample"][0, b, new].rearrange("w g d -> w (g d)"), z[r, V0:U0]).then_inc(copied, 16)
                sp.dma_start(o["pool_sample"][0, b, PREFIX - STEPS:PREFIX], z[r, U0:IN_W]).then_inc(copied, 16)
            sp.wait_ge(os_ready, 1)
            sp.dma_start(o_dram.rearrange("c p d -> p c d"), o_s).then_inc(o_st, 16)
            sp.wait_ge(o_st, 16)
            sp.wait_ge(o_done, TILES)
            by_seq = o_dram.rearrange("(h g) (i j s) d -> h i g s j d", g=KV_HEADS, i=4, s=STEPS)
            for b in range(SEQS):
                for g in range(KV_HEADS):
                    dst = mix[b * STEPS:(b + 1) * STEPS, g * GROUP * HD:(g + 1) * GROUP * HD]
                    sp.dma_start(dst.rearrange("s (j d) -> s j d", d=HD), by_seq[b // 4, b % 4, g]).then_inc(o_back, 16)
            sp.wait_ge(o_back, 16 * KV_HEADS * SEQS)
            sp.wait_ge(kv_out, 48)
            sp.wait_ge(copied, 16 * (3 + 3 * SEQS))

        @block.gpsimd
        def _(pool):
            pool.memset(resid[NS:P, SAMPLE, :], 0.0).then_inc(zeroed, 1)
            pool.wait_ge(zeroed, 1)
            pool.memset(ident[:], 0.0).then_inc(ident_set, 1)
            pool.wait_ge(ident_set, 1)
            pool.affine_select(out=ident[:], in_=ident[:], compare_op=ALU.not_equal, fill=1.0, base=0,
                               pattern=[[-1, P]], channel_multiplier=1).then_inc(ident_set, 1)
            pool.memset(kT[:, 0:P], 0.0).then_inc(zeroed, 1)
            pool.memset(v_prev[:], 0.0).then_inc(zeroed, 1)
            pool.memset(u_prev[:], 0.0).then_inc(zeroed, 1)

            pool.memset(half[:], -0.5).then_inc(zeroed, 1)
            pool.wait_ge(zeroed, 5)
            own = Chain(pool, pool_own)

            def norm_x(t, n):
                pool_after(pool, keep["passed"], sumsq, t + 1)
                rstd(own, pool, st[0:n, 1:2], st[0:n, 0:1], D, half[0:n, 0:1], x_rstd)

            def norm_mix(t, n):
                pool_after(pool, keep["passed"], mix_sq, 2 * t + 2)
                rstd(own, pool, st[0:n, 4:6], st[0:n, 2:4], ATT, half[0:n, :], m_rstd)

            def keep_previous(t):
                pool_after(pool, keep["passed"], o_done, t + 1)
                pool.tensor_copy(kT[:, 0:P], kT[:, P:2 * P]).then_inc(prev_copied, 1)
                pool.tensor_copy(v_prev[:], z[:, V0:U0]).then_inc(prev_copied, 1)
                pool.tensor_copy(u_prev[:], z[:, U0:IN_W]).then_inc(prev_copied, 1)

            norm_x(0, P)
            own.clear()
            with pool.Fori(0, LAST_PROMPT) as t:
                norm_x(t + 1, P)
                norm_mix(t, P)
                keep_previous(t)
                own.clear()
            norm_x(SAMPLE, NS)
            norm_mix(LAST_PROMPT, P)
            keep_previous(LAST_PROMPT)
            norm_mix(SAMPLE, NS)

        @block.tensor
        def _(pe):
            def transposes(n, done):
                for b in range(2):
                    for k in range(4):
                        ins = pe.transpose(X[b][:, k * n:(k + 1) * n], row[0:n, (4 * b + k) * P:(4 * b + k + 1) * P],
                                           ident[0:n, 0:n])
                    ins.then_inc(done, 1)

            def x_transposes(t, n):
                pe.wait_ge(xs_ready, t + 1)
                after(pe, mix_raw, 2 * t - 1)
                transposes(n, x_tr)

            def mix_transposes(t, n):
                pe.wait_ge(mixed, t + 1)
                transposes(n, m_tr)

            def project_in(t, n, i, weights_too=False):
                bank, n0, n1 = Z_IN[i]
                if i == 0:
                    pe.wait_ge(x_ev, 2 * t + 2)
                if weights_too:
                    pe.wait_ge(win_ld[i], 16)
                for k in range(KC):
                    ins = pe.matmul(bank[0:n, 0:n1 - n0], colT[:, k, 0:n], w_in[:, k, n0:n1],
                                    start=(k == 0), stop=(k == KC - 1))
                ins.then_inc(z_done, 1)

            def pool_means(t, n, prev, prev_mat, cur_mat):
                pe.wait_ge(zk_ev, 2 * t + 2)
                after(pe, prev_copied, 3 * t)
                after(pe, added[0], t)
                for g in range(PG):
                    out = Z[0][:, g * n:(g + 1) * n]
                    pe.matmul(out, prev[:, g * P:(g + 1) * P], prev_mat(g), start=True, stop=False)
                    ins = pe.matmul(out, z[0:n, U0 + g * P:U0 + (g + 1) * P], cur_mat(g), start=False, stop=True)
                ins.then_inc(d_done, 1)

            def qk_transposes(t, n):
                pe.wait_ge(roped, t + 1)
                after(pe, m_ev, 2 * t)
                for j in range(GROUP):
                    pe.transpose(X[0][:, j * n:(j + 1) * n], z[0:n, j * P:(j + 1) * P], ident[0:n, 0:n])
                pe.transpose(X[1][:, 0:n], z[0:n, K0:V0], ident[0:n, 0:n]).then_inc(qk_tr, 1)

            def pool_map(t, n):
                pe.wait_ge(dT_ev, t + 1)
                for g in range(PG):
                    ins = pe.matmul(X[0][0:n, g * P:(g + 1) * P], dT[:, g, 0:n] if n == P else
                                    dT[:].rearrange("p g q -> p (g q)")[:, g * n:(g + 1) * n],
                                    w_pool[:, g, :], start=True, stop=True)
                ins.then_inc(y_done, 1)

            def project_out(t, n, half):
                pe.wait_ge(m_ev, 2 * t + 2)
                if isinstance(t, int):
                    after(pe, added[half], t)
                for k in range(KC):
                    ins = pe.matmul(Z[half][0:n, :], colM[:, k, 0:n], w_out[:, k, half * 512:(half + 1) * 512],
                                    start=(k == 0), stop=(k == KC - 1))
                ins.then_inc(proj_done[half], 1)

            def prompt_tile(t, cur, n_next):
                qk_transposes(t, P)
                if isinstance(t, int) and t == 0:
                    pe.wait_ge(c_ld, 16 * NCONST)
                    pe.wait_ge(zeroed, 4)
                pool_means(t, P, u_prev, lambda g: pmat[:, 2, g, :], lambda g: pmat[:, cur, g, :])
                pe.wait_ge(qk_ev, 2 * t + 2)
                after(pe, pt_act, 2 * t)
                after(pe, pt_dve, 2 * t)
                for h in range(HEADS):
                    g, j = divmod(h, GROUP)
                    ins = pe.matmul(S[h // 2][:, (h % 2) * 256:(h % 2) * 256 + 256],
                                    qT[HD * g:HD * g + HD, j, :], kT[HD * g:HD * g + HD, :], start=True, stop=True)
                    if h % 2:
                        ins.then_inc(s_done, 1)
                pool_map(t, P)
                if not (isinstance(t, int) and t == 0):
                    project_out(t - 1, P, 1)
                for h in range(HEADS):
                    if h % 2 == 0:
                        pe.wait_ge(p_ready, 4 * t + h // 2 + 1)
                    for b in range(2):
                        ins = pe.transpose(S[h // 2][:, (h % 2) * 256 + b * P:(h % 2) * 256 + (b + 1) * P],
                                           prob[:, h, b * P:(b + 1) * P], ident[:])
                    if h % 2:
                        ins.then_inc(pt_tr, 1)
                x_transposes(t + 1, n_next)
                pe.wait_ge(pt_dve, 2 * t + 2)
                pe.wait_ge(pt_act, 2 * t + 2)
                for h in range(HEADS):
                    g = h // GROUP
                    out = Z[0][:, h * HD:(h + 1) * HD]
                    pe.matmul(out, probT[:, h, 0, :], v_prev[:, g * HD:(g + 1) * HD], start=True, stop=False)
                    ins = pe.matmul(out, probT[:, h, 1, :], z[:, V0 + g * HD:V0 + (g + 1) * HD],
                                    start=False, stop=True)
                ins.then_inc(o_done, 1)
                project_in(t + 1, n_next, 0)
                project_in(t + 1, n_next, 1)
                mix_transposes(t, P)
                project_in(t + 1, n_next, 2)
                if isinstance(t, int) and t == 0:
                    pe.wait_ge(wout_ld, 16)
                project_out(t, P, 0)

            def sample_tile(t):
                n = NS
                nst = SEQS * PREFIX
                pe.wait_ge(late_ld, 16 * 4)
                pe.wait_ge(zk_ev, 2 * t + 2)
                pe.wait_ge(cache_ld, 32)
                for b in range(SEQS):
                    ins = pe.transpose(S[2 + b // 4][:, (b % 4) * P:(b % 4 + 1) * P], kc[:, b, :], ident[:])
                ins.then_inc(kc_tr, 1)
                qk_transposes(t, n)
                pool_means(t, n, ustate, lambda g: pmat_s[0:nst, 1, g, :], lambda g: pmat_s[0:n, 0, g, :])
                pe.wait_ge(qk_ev, 2 * t + 2)
                pe.wait_ge(kc_ev, 2)
                for ch in range(4):
                    half, g = divmod(ch, KV_HEADS)
                    for i in range(4):
                        b = 4 * half + i
                        q = qT[:].rearrange("p j q -> p (j q)")[HD * g:HD * g + HD, 32 * b:32 * b + 32]
                        rows = slice(32 * i, 32 * i + 32)
                        pe.matmul(S[ch][rows, 0:P], q, kcT[HD * g:HD * g + HD, b, :], start=True, stop=True)
                        ins = pe.matmul(S[ch][rows, P:P + n], q, kT[HD * g:HD * g + HD, P:P + n],
                                        start=True, stop=True)
                    ins.then_inc(s_done, 1)
                pool_map(t, n)
                project_out(t - 1, P, 1)
                pe.wait_ge(p_ready, 4 * t + 4)
                for ch in range(4):
                    pe.transpose(S[ch][:, 0:P], prob_s[:, ch, 0:P], ident[:])
                    ins = pe.transpose(S[ch][0:n, P:2 * P], prob_s[:, ch, P:P + n], ident[:])
                    ins.then_inc(pt_tr, 1)
                pe.wait_ge(pts_ev, 9)
                for ch in range(4):
                    half, g = divmod(ch, KV_HEADS)
                    for i in range(4):
                        out = Z[0][32 * i:32 * i + 32, ch * HD:(ch + 1) * HD]
                        pe.matmul(out, ptc[:, ch, 32 * i:32 * i + 32], vc[:, 4 * half + i, g * HD:(g + 1) * HD],
                                  start=True, stop=False)
                        ins = pe.matmul(out, ptn[0:n, ch, 32 * i:32 * i + 32], z[0:n, V0 + g * HD:V0 + (g + 1) * HD],
                                        start=False, stop=True)
                ins.then_inc(o_done, 1)
                mix_transposes(t, n)
                project_out(t, n, 0)
                project_out(t, n, 1)

            pe.wait_ge(ident_set, 2)
            x_transposes(0, P)
            for i in range(3):
                project_in(0, P, i, weights_too=True)
            prompt_tile(0, 0, P)
            with pe.Fori(1, LAST_PROMPT) as t:
                prompt_tile(t, 1, P)
            prompt_tile(LAST_PROMPT, 1, NS)
            sample_tile(SAMPLE)

        @block.scalar
        def _(act):
            def square_sum(t, n, src):
                after(act, xs_ready, t)
                after(act, mix_sq, 2 * t - 2)
                act.activation(junk[0:n, :], src, ACT.Square, accum_out=st[0:n, 0:1]).then_inc(sumsq, 1)

            def col_copy(dst, t, n, tr, ev):
                act.wait_ge(tr, 2 * t + 1)
                act.activation(dst[:, 0:4, 0:n], X[0][:, 0:4 * n].rearrange("p (k q) -> p k q", k=4),
                               ACT.Copy).then_inc(ev, 1)

            def z_copy(t, n, i):
                bank, n0, n1 = Z_IN[i]
                if i == 1:
                    after(act, prev_copied, 3 * t)
                act.wait_ge(z_done, 3 * t + i + 1)
                act.activation(z[0:n, n0:n1], bank[0:n, 0:n1 - n0], ACT.Copy).then_inc(zk_ev, 1)

            def dT_copy(t, n):
                act.wait_ge(d_done, t + 1)
                act.activation(dT[:].rearrange("p g q -> p (g q)")[:, 0:PG * n], Z[0][:, 0:PG * n],
                               ACT.Copy).then_inc(dT_ev, 1)

            def k_copy(t, n):
                act.wait_ge(qk_tr, t + 1)
                act.activation(kT[:, P:P + n], X[1][:, 0:n], ACT.Copy).then_inc(qk_ev, 1)

            def mix_squares(t, n):
                act.wait_ge(mix_raw, 2 * t + (2 if n == P else 1))
                act.wait_ge(sumsq, t + 2 if n == P else TILES)
                after(act, mixed, t)
                act.activation(junk[0:n, 0:ATT], mix[0:n, 0:ATT], ACT.Square, accum_out=st[0:n, 2:3]).then_inc(mix_sq, 1)
                act.activation(junk[0:n, ATT:D], mix[0:n, ATT:D], ACT.Square, accum_out=st[0:n, 3:4]).then_inc(mix_sq, 1)

            def prompt_tile(t, next_src, n_next):
                k_copy(t, P)
                dT_copy(t, P)
                square_sum(t + 1, n_next, next_src)
                act.wait_ge(m_ready, t + 1)
                for h in range(HEADS):
                    ins = act.activation(prob[:, h, :], prob[:, h, :], ACT.Exp, bias=m8[:, 1, h:h + 1],
                                         accum_out=den[:, h:h + 1])
                    if h == HEADS - 1:
                        act.activation(m8[:, 2, :], m8[:, 2, :], ACT.Exp).then_inc(p_ready, 1)
                    elif h % 2:
                        ins.then_inc(p_ready, 1)
                for b in (2, 3):
                    act.wait_ge(pt_tr, 4 * t + b + 1)
                    act.activation(probT[:, 2 * b:2 * b + 2].rearrange("p h b q -> p (h b q)"), S[b][:],
                                   ACT.Copy).then_inc(pt_act, 1)
                col_copy(colT, t + 1, n_next, x_tr, x_ev)
                mix_squares(t, P)
                if n_next == NS:
                    act.wait_ge(kv_out, 48)
                z_copy(t + 1, n_next, 1)
                col_copy(colM, t, P, m_tr, m_ev)
                z_copy(t + 1, n_next, 2)

            def sample_tile(t):
                n = NS
                act.wait_ge(kc_tr, 1)
                for i in range(2):
                    act.activation(kcT[:, 4 * i:4 * i + 4, :].rearrange("p b k -> p (b k)"), S[2 + i][:],
                                   ACT.Copy).then_inc(kc_ev, 1)
                k_copy(t, n)
                dT_copy(t, n)
                act.wait_ge(m_ready, t + 1)
                for ch in range(4):
                    act.activation(prob_s[:, ch, :], prob_s[:, ch, :], ACT.Exp, bias=m8[:, 1, ch:ch + 1],
                                   accum_out=den[:, ch:ch + 1]).then_inc(p_ready, 1)
                act.activation(m8[:, 2, 0:4], m8[:, 2, 0:4], ACT.Exp).then_inc(pts_ev, 1)
                for ch in range(4):
                    act.wait_ge(pt_tr, 4 * t + ch + 1)
                    act.activation(ptc[:, ch, :], S[ch][:, 0:P], ACT.Copy).then_inc(pts_ev, 1)
                    act.activation(ptn[0:n, ch, :], S[ch][0:n, P:2 * P], ACT.Copy).then_inc(pts_ev, 1)
                act.wait_ge(o_back, 16 * KV_HEADS * SEQS)
                mix_squares(t, n)
                col_copy(colM, t, n, m_tr, m_ev)

            act.wait_ge(x0_ld, 16)
            square_sum(0, P, resid[:, 0, :])
            col_copy(colT, 0, P, x_tr, x_ev)
            z_copy(0, P, 1)
            z_copy(0, P, 2)
            act.wait_ge(x_ld, 32)
            prompt_tile(0, resid[:, 1, :], P)
            with act.Fori(1, LAST_PROMPT) as t:
                prompt_tile(t, resid[:, t + 1, :], P)
            prompt_tile(LAST_PROMPT, resid[0:NS, SAMPLE, :], NS)
            sample_tile(SAMPLE)

        @block.vector
        def _(dve):
            own = Chain(dve, dve_own)

            def norm_in(t, n, src):
                dve.wait_ge(x_rstd, t + 1)
                after(dve, m_tr, 2 * t - 2)
                dve.scalar_tensor_tensor(out=row[0:n, :].rearrange("p (k q) -> p q k", k=KC),
                                         in0=src.rearrange("p (q k) -> p q k", k=KC), scalar=st[0:n, 1:2],
                                         in1=g_mix[0:n, :].rearrange("p (q k) -> p q k", k=KC),
                                         op0=ALU.mult, op1=ALU.mult).then_inc(xs_ready, 1)

            def col_copy(dst, t, n, tr, ev):
                dve.wait_ge(tr, 2 * t + 2)
                dve.tensor_copy(dst[:, 4:8, 0:n],
                                X[1][:, 0:4 * n].rearrange("p (k q) -> p k q", k=4)).then_inc(ev, 1)

            def rotate(t, n):
                dve.wait_ge(z_done, 3 * t + 1)
                own.did(dve.tensor_copy(z[0:n, 0:ATT].rearrange("p (j g d) -> p g j d", j=GROUP, d=HD),
                                        Z_IN[0][0][0:n, :].rearrange("p (g j d) -> p g j d", j=GROUP, d=HD)))
                own.wait()
                dve.wait_ge(zk_ev, 2 * t + 1)
                heads = HEADS + KV_HEADS
                hv = z[0:n, 0:V0].rearrange("p (h d) -> p h d", d=HD)
                x1, x2 = hv[:, :, 0:HALF], hv[:, :, HALF:2 * HALF]
                cs = [rope[0:n, t, i:i + 1, :].broadcast_to([n, heads, HALF]) for i in range(2)]
                for i, (x, f) in enumerate(((x1, 0), (x2, 1), (x2, 0), (x1, 1))):
                    own.did(dve.tensor_tensor(rt[0:n, i], x, cs[f], ALU.mult))
                own.wait()
                own.did(dve.tensor_tensor(x1, rt[0:n, 0], rt[0:n, 1], ALU.subtract))
                dve.tensor_tensor(x2, rt[0:n, 2], rt[0:n, 3], ALU.add).then_inc(roped, 1)

            def q_copy(t, n):
                dve.wait_ge(qk_tr, t + 1)
                dst, src = qT[:].rearrange("p j q -> p (j q)")[:, 0:GROUP * n], X[0][:, 0:GROUP * n]
                if n != P:
                    dst = dst.rearrange("p (b j s) -> p j b s", j=GROUP, s=STEPS)
                    src = src.rearrange("p (j b s) -> p j b s", j=GROUP, s=STEPS)
                dve.tensor_copy(dst, src).then_inc(qk_ev, 1)

            def softmax_head(t, n_sets, sinks):
                own.wait()
                own.did(dve.tensor_tensor(m8[:, 0, 0:n_sets], mx[:, 0:n_sets], sinks, ALU.max))
                own.wait()
                own.did(dve.tensor_tensor(m8[:, 2, 0:n_sets], sinks, m8[:, 0, 0:n_sets], ALU.subtract))
                own.wait()
                dve.tensor_scalar(m8[:, 1, 0:n_sets], m8[:, 0, 0:n_sets], -1.0, None, ALU.mult).then_inc(m_ready, 1)

            def denominators(n_sets):
                own.did(dve.tensor_tensor(den[:, 0:n_sets], den[:, 0:n_sets], m8[:, 2, 0:n_sets], ALU.add))
                own.wait()
                own.did(dve.reciprocal(rden[:, 0:n_sets], den[:, 0:n_sets]))
                own.wait()

            def pool_scale(t, n):
                dve.wait_ge(y_done, t + 1)
                dve.tensor_tensor(mix[0:n, ATT:D], X[0][0:n, :], p_scale[0:n, :], ALU.mult).then_inc(mix_raw, 1)

            def mix_norm(t, n):
                dve.wait_ge(m_rstd, t + 1)
                for i in range(2):
                    w = slice(i * ATT, (i + 1) * ATT)
                    ins = dve.scalar_tensor_tensor(
                        out=row[0:n, :].rearrange("p (k q) -> p q k", k=KC)[:, i * 64:(i + 1) * 64, :],
                        in0=mix[0:n, w].rearrange("p (q k) -> p q k", k=KC), scalar=st[0:n, 4 + i:5 + i],
                        in1=g_mid[0:n, w].rearrange("p (q k) -> p q k", k=KC), op0=ALU.mult, op1=ALU.mult)
                    if i == 0:
                        own.did(ins)
                own.wait()
                ins.then_inc(mixed, 1)

            def add_residual(n, dst, done, half):
                dve.wait_ge(proj_done[half], done)
                w = slice(half * 512, (half + 1) * 512)
                dve.tensor_tensor(dst[:, w], Z[half][0:n, :], dst[:, w], ALU.add).then_inc(added[half], 1)

            def prompt_tile(t, mask, next_src, n_next):
                q_copy(t, P)
                for b in range(4):
                    dve.wait_ge(s_done, 4 * t + b + 1)
                    own.did(dve.scalar_tensor_tensor(
                        out=prob[:, 2 * b:2 * b + 2, :], in0=S[b][:].rearrange("p (h k) -> p h k", h=2), scalar=SCALE,
                        in1=amask[:, mask:mask + 1, :].broadcast_to([P, 2, 2 * P]), op0=ALU.mult, op1=ALU.add))
                    own.wait()
                    own.did(dve.tensor_reduce(mx[:, 2 * b:2 * b + 2], prob[:, 2 * b:2 * b + 2, :], AX.X, ALU.max))
                softmax_head(t, HEADS, sink[:])
                norm_in(t + 1, n_next, next_src)
                pool_scale(t, P)
                if not (isinstance(t, int) and t == 0):
                    add_residual(P, resid[:, t - 1, :], t, 1)
                for b in (0, 1):
                    dve.wait_ge(pt_tr, 4 * t + b + 1)
                    dve.tensor_copy(probT[:, 2 * b:2 * b + 2].rearrange("p h b q -> p (h b q)"),
                                    S[b][:]).then_inc(pt_dve, 1)
                dve.wait_ge(p_ready, 4 * t + 4)
                denominators(HEADS)
                col_copy(colT, t + 1, n_next, x_tr, x_ev)
                dve.wait_ge(o_done, t + 1)
                dve.tensor_tensor(mix[:, 0:ATT].rearrange("p (h d) -> p h d", d=HD),
                                  Z[0][:].rearrange("p (h d) -> p h d", d=HD),
                                  rden[:, :].rearrange("p (h q) -> p h q", q=1).broadcast_to([P, HEADS, HD]),
                                  ALU.mult).then_inc(mix_raw, 1)
                mix_norm(t, P)
                col_copy(colM, t, P, m_tr, m_ev)
                if n_next == NS:
                    dve.wait_ge(kv_out, 48)
                rotate(t + 1, n_next)
                add_residual(P, resid[:, t, :], t + 1, 0)
                own.clear()

            def sample_tile(t):
                n = NS
                q_copy(t, n)
                for ch in range(4):
                    dve.wait_ge(s_done, 4 * t + ch + 1)
                    own.did(dve.scalar_tensor_tensor(out=prob_s[:, ch, :], in0=S[ch][:, 0:P + n], scalar=SCALE,
                                                     in1=smask[:, ch // 2, :], op0=ALU.mult, op1=ALU.add))
                    own.wait()
                    own.did(dve.tensor_reduce(mx[:, ch:ch + 1], prob_s[:, ch, :], AX.X, ALU.max))
                own.did(dve.tensor_tensor(picked[:], pick[:], sink[:, :].rearrange("p (a h) -> p a h", a=1).broadcast_to(
                    [P, KV_HEADS, HEADS]), ALU.mult))
                own.wait()
                own.did(dve.tensor_reduce(sink_s[:], picked[:], AX.X, ALU.add))
                own.wait()
                for half in range(2):
                    own.did(dve.tensor_copy(m8[:, 1, 2 * half:2 * half + 2], sink_s[:]))
                own.wait()
                own.did(dve.tensor_tensor(m8[:, 0, 0:4], mx[:, 0:4], m8[:, 1, 0:4], ALU.max))
                own.wait()
                own.did(dve.tensor_tensor(m8[:, 2, 0:4], m8[:, 1, 0:4], m8[:, 0, 0:4], ALU.subtract))
                own.wait()
                dve.tensor_scalar(m8[:, 1, 0:4], m8[:, 0, 0:4], -1.0, None, ALU.mult).then_inc(m_ready, 1)
                pool_scale(t, n)
                add_residual(P, resid[:, t - 1, :], t, 1)
                dve.wait_ge(pts_ev, 9)
                denominators(4)
                dve.wait_ge(o_done, t + 1)
                dve.tensor_tensor(o_s, Z[0][:, 0:4 * HD].rearrange("p (c d) -> p c d", c=4),
                                  rden[:, 0:4].rearrange("p (c q) -> p c q", q=1).broadcast_to([P, 4, HD]),
                                  ALU.mult).then_inc(os_ready, 1)
                dve.wait_ge(o_back, 16 * KV_HEADS * SEQS)
                mix_norm(t, n)
                col_copy(colM, t, n, m_tr, m_ev)
                for half in range(2):
                    add_residual(n, resid[0:n, t, :], t + 1, half)

            dve.wait_ge(x0_ld, 16)
            dve.wait_ge(g_mix_ld, 16)
            norm_in(0, P, resid[:, 0, :])
            col_copy(colT, 0, P, x_tr, x_ev)
            dve.wait_ge(c_ld, 16 * NCONST)
            rotate(0, P)
            dve.wait_ge(x_ld, 32)
            own.clear()
            prompt_tile(0, 0, resid[:, 1, :], P)
            with dve.Fori(1, LAST_PROMPT) as t:
                prompt_tile(t, 1, resid[:, t + 1, :], P)
            dve.wait_ge(zeroed, 4)
            dve.wait_ge(late_ld, 16 * 4)
            prompt_tile(LAST_PROMPT, 1, resid[0:NS, SAMPLE, :], NS)
            sample_tile(SAMPLE)




def router(nc, a, c, keep, rows_dram, y_dram):
    resid, ident, place, w8, slots, rounds, y_row = (
        keep[n] for n in ("resid", "ident", "place", "w8", "slots", "rounds", "y_row"))
    LAST = TILES - 1
    with ExitStack() as ctx:
        def sb(name, shape, dt=F32):
            return ctx.enter_context(nc.sbuf_tensor(name, shape, dt))

        def sem(name):
            return ctx.enter_context(nc.semaphore(name))

        w_r = sb("w_r", [P, KC, E])
        s_gate = sb("s_gate", [P, KC, FE])
        s_up = sb("s_up", [P, KC, FE])
        s_down = sb("s_down", [P, FC, D])
        g_ffn = sb("g_ffn", [P, D])
        bias = sb("bias", [P, E])
        tri_f = sb("tri_f", [P, P])
        tri = sb("tri", [P, P], BF16)
        ones = sb("ones", [P, P], BF16)
        iota_e = sb("iota_e", [P, E])
        valid = sb("valid", [P, TILES])
        row = sb("row2", [P, D])
        colT = sb("colT2", [P, KC, P])
        junk = sb("junk2", [P, D], BF16)
        st = sb("st2", [P, 4])
        half = sb("half2", [P, 1])
        zero = sb("zero", [P, D])
        sg = sb("sg", [P, 3, 2 * P])
        hid = sb("hid", [P, FC, P])
        score = sb("score", [P, E])
        biased = sb("biased", [P, E])
        top2 = sb("top2", [P, EG, 8])
        grp = sb("grp", [P, EG])
        gv = sb("gv", [P, 8])
        gi = sb("gi", [P, 8], U32)
        gif = sb("gif", [P, 8])
        geq = sb("geq", [P, EG, TOP_GROUPS])
        pen = sb("pen", [P, EG])
        v8 = sb("v8", [P, 8])
        i8 = sb("i8", [P, 8], U32)
        idx8 = sb("idx8", [P, TILES, TOP])
        pos8 = sb("pos8", [P, TILES, TOP])
        hot = sb("hot", [P, TOP, E])
        prod = sb("prod", [P, TOP, E])
        maskf = sb("maskf", [P, E])
        maskb = sb("maskb", [P, E], BF16)
        sofar = sb("sofar", [P, E], BF16)
        pe_pos = sb("pe_pos", [P, E])
        sel8 = sb("sel8", [P, TOP])
        sums = sb("sums", [P, 2])
        tmp = sb("tmp", [P, 2, TILES * TOP])
        top = sb("top", [1, 2])
        cnt = sb("cnt", [1, 6, E])
        one_f = sb("one_f", [1, P])
        shift = sb("shift", [P, E])

        X = [ctx.enter_context(nc.psum_tensor(f"RX{i}", [P, 512], F32)) for i in range(2)]
        R, G, U, C = (ctx.enter_context(nc.psum_tensor(n, [P, 512], F32)) for n in ("RR", "RG", "RU", "RC"))
        Y = [ctx.enter_context(nc.psum_tensor(f"RY{i}", [P, 512], F32)) for i in range(2)]

        w_ld, sumsq, row_ready, row_st, x_tr, x_ev, r_done, g_done, u_done, e_ready, s_ready, h_ready, y_done = (
            sem(n) for n in ("w_ld2", "sumsq2", "row_ready", "row_st", "x_tr2", "x_ev2", "r_done", "g_done", "u_done",
                             "e_ready", "s_ready", "h_ready2", "y_done2"))
        y_added, mask_ready, placed, consts, count_done = (
            sem(n) for n in ("y_added", "mask_ready", "placed", "consts2", "count_done"))
        shift_ready, rounds_known, cleared = sem("shift_ready"), sem("rounds_known"), sem("cleared")
        dve_own, pool_own, rstd_ready = sem("dve_own_router"), sem("pool_own_router"), sem("rstd_ready2")

        block = ctx.enter_context(nc.Block())

        @block.sync
        def _(sp):
            for dst, src in ((g_ffn[:], a["g_ffn"][0:1, :].broadcast_to([P, D])),
                             (w_r[:], a["w_router"][0].rearrange("(p k) e -> p k e", k=KC)),
                             (s_gate[:], a["w_sh_gate"][0].rearrange("(p k) f -> p k f", k=KC)),
                             (s_up[:], a["w_sh_up"][0].rearrange("(p k) f -> p k f", k=KC)),
                             (s_down[:], a["w_sh_down"][0].rearrange("(f p) d -> p f d", p=P)),
                             (bias[:], a["router_bias"][0:1, :].broadcast_to([P, E])),
                             (tri_f[:], c["tri"]), (iota_e[:], c["iota_e"]), (valid[:], c["valid"])):
                sp.dma_start(dst, src).then_inc(w_ld, 16)
            sp.dma_start(keep["raw_d"][:], a["w_exp_down"][0, 0].rearrange("(f p) d -> p f d", p=P)).then_inc(
                keep["d_ld"], 16)
            with sp.Fori(0, TILES) as t:
                at = sp.snap(t * P)
                sp.wait_ge(row_ready, t + 1)
                sp.dma_start(rows_dram[bass.ds(at, P)], row[:]).then_inc(row_st, 16)
            sp.wait_ge(row_st, 16 * TILES)
            sp.wait_ge(rounds_known, 1)
            n_rounds = sp.value_load(rounds[0:1, 0:1], min_val=1, max_val=ROUNDS)
            with sp.If(n_rounds > 1):
                whole = (Y_ROWS - OVER_ROW) // P
                with sp.Fori(0, whole) as i:
                    at = sp.snap(i * P + OVER_ROW)
                    sp.dma_start(y_dram[bass.ds(at, P)], zero[:]).then_inc(cleared, 16)
                rest = Y_ROWS - OVER_ROW - whole * P
                sp.dma_start(y_dram[Y_ROWS - rest:Y_ROWS], zero[0:rest, :]).then_inc(cleared, 16)
                sp.wait_ge(cleared, 16 * whole + 16)

        @block.gpsimd
        def _(pool):
            pool.memset(ones[:], 1.0).then_inc(consts, 1)
            pool.memset(sofar[:], 0.0).then_inc(consts, 1)
            pool.memset(place[:, E:E + 3, :], 0.0).then_inc(consts, 1)
            pool.memset(half[:], -0.5).then_inc(consts, 1)
            pool.memset(zero[:], 0.0).then_inc(consts, 1)
            pool.wait_ge(consts, 5)
            own = Chain(pool, pool_own)
            with pool.Fori(0, TILES) as t:
                pool_after(pool, keep["passed"], sumsq, t + 1)
                rstd(own, pool, st[:, 2:3], st[:, 0:1], D, half[:], rstd_ready)
                own.clear()

        @block.tensor
        def _(pe):
            def tile(t):
                pe.wait_ge(row_ready, t + 1)
                after(pe, x_ev, 2 * t)
                for b in range(2):
                    for k in range(4):
                        ins = pe.transpose(X[b][:, k * P:(k + 1) * P], row[:, (4 * b + k) * P:(4 * b + k + 1) * P],
                                           ident[:])
                    ins.then_inc(x_tr, 1)
                pe.wait_ge(x_ev, 2 * t + 2)
                after(pe, s_ready, t)
                for k in range(KC):
                    ins = pe.matmul(R[:, 0:E], colT[:, k, :], w_r[:, k, :], start=(k == 0), stop=(k == KC - 1))
                ins.then_inc(r_done, 1)
                after(pe, h_ready, t)
                for bank, w, done in ((G, s_gate, g_done), (U, s_up, u_done)):
                    for f in range(FC):
                        for k in range(KC):
                            ins = pe.matmul(bank[:, f * P:(f + 1) * P], w[:, k, f * P:(f + 1) * P], colT[:, k, :],
                                            start=(k == 0), stop=(k == KC - 1))
                    ins.then_inc(done, 1)
                pe.wait_ge(mask_ready, t + 1)
                after(pe, placed, t)
                pe.matmul(C[:, 0:E], tri[:], maskb[:], start=True, stop=False)
                pe.matmul(C[:, 0:E], ones[:], sofar[:], start=False, stop=True).then_inc(count_done, 1)
                pe.wait_ge(h_ready, t + 1)
                after(pe, y_added, 2 * t)
                for half in range(2):
                    for f in range(FC):
                        ins = pe.matmul(Y[half][:], hid[:, f, :], s_down[:, f, half * 512:(half + 1) * 512],
                                        start=(f == 0), stop=(f == FC - 1))
                    ins.then_inc(y_done, 1)

            pe.wait_ge(w_ld, 16 * 9)
            pe.wait_ge(consts, 5)
            tile(0)
            with pe.Fori(1, TILES) as t:
                tile(t)
            pe.wait_ge(placed, TILES)
            pe.matmul(C[0:1, 0:E], ones[:, 0:1], sofar[:], start=True, stop=True).then_inc(count_done, 1)
            pe.wait_ge(shift_ready, 1)
            pe.matmul(C[:, 0:E], one_f[:], cnt[:, 5, :], start=True, stop=True).then_inc(count_done, 1)

        @block.scalar
        def _(act):
            def square_sum(t):
                act.activation(junk[:], resid[:, t, :], ACT.Square, accum_out=st[:, 0:1]).then_inc(sumsq, 1)

            def tile(t, then):
                act.wait_ge(x_tr, 2 * t + 1)
                act.activation(colT[:, 0:4, :], X[0][:].rearrange("p (k q) -> p k q", k=4),
                               ACT.Copy).then_inc(x_ev, 1)
                act.wait_ge(row_ready, t + 1)
                then()
                act.wait_ge(r_done, t + 1)
                act.activation(score[:], R[:, 0:E], ACT.Exp, scale=-1.0).then_inc(e_ready, 1)
                act.wait_ge(g_done, t + 1)
                act.activation(sg[:, 0, :], G[:, 0:FC * P], ACT.Exp, scale=-1.0).then_inc(e_ready, 1)

            square_sum(0)
            tile(0, lambda: square_sum(1))
            with act.Fori(1, LAST) as t:
                tile(t, lambda: square_sum(t + 1))
            tile(LAST, lambda: None)

        @block.vector
        def _(dve):
            own = Chain(dve, dve_own)

            def norm(t):
                dve.wait_ge(rstd_ready, t + 1)
                after(dve, row_st, 16 * t)
                dve.scalar_tensor_tensor(out=row[:].rearrange("p (k q) -> p q k", k=KC),
                                         in0=resid[:, t, :].rearrange("p (q k) -> p q k", k=KC), scalar=st[:, 2:3],
                                         in1=g_ffn[:].rearrange("p (q k) -> p q k", k=KC),
                                         op0=ALU.mult, op1=ALU.mult).then_inc(row_ready, 1)

            def hot_sum(factor, dst):
                own.did(dve.tensor_tensor(prod[:], hot[:], factor.rearrange("p (a e) -> p a e", a=1).broadcast_to(
                    [P, TOP, E]), ALU.mult))
                own.wait()
                own.did(dve.tensor_reduce(dst, prod[:], AX.X, ALU.add))
                own.wait()

            def choose(t):
                dve.wait_ge(e_ready, 2 * t + 1)
                own.did(dve.tensor_scalar(score[:], score[:], 1.0, None, ALU.add))
                own.wait()
                own.did(dve.reciprocal(score[:], score[:]))
                own.wait()
                own.did(dve.tensor_tensor(biased[:], score[:], bias[:], ALU.add))
                own.wait()
                for g in range(EG):
                    own.did(dve.max(top2[:, g, :], biased[:, g * EG:(g + 1) * EG]))
                own.wait()
                own.did(dve.tensor_tensor(grp[:], top2[:, :, 0], top2[:, :, 1], ALU.add))
                own.wait()
                own.did(dve.max(gv[:], grp[:]))
                own.wait()
                own.did(dve.max_index(gi[:], gv[:], grp[:]))
                own.wait()
                own.did(dve.tensor_copy(gif[:], gi[:]))
                own.wait()
                own.did(dve.tensor_tensor(
                    geq[:], iota_e[:, 0:EG].rearrange("p (g k) -> p g k", k=1).broadcast_to([P, EG, TOP_GROUPS]),
                    gif[:, 0:TOP_GROUPS].rearrange("p (a k) -> p a k", a=1).broadcast_to([P, EG, TOP_GROUPS]),
                    ALU.is_equal))
                own.wait()
                own.did(dve.tensor_reduce(pen[:], geq[:], AX.X, ALU.add))
                own.wait()
                own.did(dve.tensor_scalar(pen[:], pen[:], -NEG, NEG, ALU.mult, ALU.add))
                own.wait()
                own.did(dve.tensor_tensor(
                    biased[:].rearrange("p (g e) -> p g e", g=EG), biased[:].rearrange("p (g e) -> p g e", g=EG),
                    pen[:].rearrange("p (g e) -> p g e", e=1).broadcast_to([P, EG, E // EG]), ALU.add))
                own.wait()
                own.did(dve.max(v8[:], biased[:]))
                own.wait()
                own.did(dve.max_index(i8[:], v8[:], biased[:]))
                own.wait()
                own.did(dve.tensor_copy(idx8[:, t, :], i8[:]))
                own.wait()
                own.did(dve.tensor_tensor(
                    hot[:], iota_e[:].rearrange("p (a e) -> p a e", a=1).broadcast_to([P, TOP, E]),
                    idx8[:, t, :].rearrange("p (k e) -> p k e", e=1).broadcast_to([P, TOP, E]), ALU.is_equal))
                own.wait()
                own.did(dve.tensor_reduce(maskf[:], hot[:].rearrange("p k e -> p e k"), AX.X, ALU.add))
                own.wait()
                own.did(dve.tensor_scalar(maskf[:], maskf[:], valid[:, bass.ds(t, 1)], None, ALU.mult))
                own.wait()
                dve.tensor_copy(maskb[:], maskf[:]).then_inc(mask_ready, 1)

            def weights(t):
                hot_sum(score[:], sel8[:])
                own.did(dve.tensor_reduce(sums[:, 0:1], sel8[:], AX.X, ALU.add))
                own.wait()
                own.did(dve.reciprocal(sums[:, 1:2], sums[:, 0:1]))
                own.wait()
                dve.tensor_scalar(w8[:, t, :], sel8[:], sums[:, 1:2], ROUTED_SCALE, ALU.mult,
                                  ALU.mult).then_inc(s_ready, 1)

            def places(t):
                dve.wait_ge(count_done, t + 1)
                own.did(dve.scalar_tensor_tensor(out=pe_pos[:], in0=C[:, 0:E], scalar=1.0, in1=maskf[:],
                                                 op0=ALU.add, op1=ALU.mult))
                own.wait()
                own.did(dve.tensor_copy(place[:, 0:E, t], pe_pos[:]))
                own.did(dve.tensor_tensor(sofar[:], sofar[:], maskf[:], ALU.add))
                hot_sum(pe_pos[:], pos8[:, t, :])
                own.wait()
                dve.tensor_copy(sums[:, 0:1], sums[:, 1:2]).then_inc(placed, 1)

            def shared(t):
                dve.wait_ge(e_ready, 2 * t + 2)
                own.did(dve.tensor_scalar(sg[:, 1, :], sg[:, 0, :], 1.0, None, ALU.add))
                own.wait()
                own.did(dve.reciprocal(sg[:, 2, :], sg[:, 1, :]))
                own.wait()
                own.did(dve.tensor_tensor(sg[:, 1, :], sg[:, 2, :], G[:, 0:FC * P], ALU.mult))
                own.wait()
                dve.wait_ge(u_done, t + 1)
                dve.tensor_tensor(hid[:].rearrange("p f q -> p (f q)"), sg[:, 1, :], U[:, 0:FC * P],
                                  ALU.mult).then_inc(h_ready, 1)

            def tile(t, then):
                dve.wait_ge(x_tr, 2 * t + 2)
                dve.tensor_copy(colT[:, 4:8, :], X[1][:].rearrange("p (k q) -> p k q", k=4)).then_inc(x_ev, 1)
                choose(t)
                shared(t)
                then()
                weights(t)
                places(t)
                for half in range(2):
                    dve.wait_ge(y_done, 2 * t + half + 1)
                    w = slice(half * 512, (half + 1) * 512)
                    dve.tensor_tensor(resid[:, t, w], Y[half][:], resid[:, t, w], ALU.add).then_inc(y_added, 1)
                own.clear()

            dve.wait_ge(w_ld, 16 * 9)
            dve.wait_ge(consts, 5)
            own.did(dve.tensor_copy(tri[:], tri_f[:]))
            own.wait()
            norm(0)
            tile(0, lambda: norm(1))
            with dve.Fori(1, LAST) as t:
                tile(t, lambda: norm(t + 1))
            tile(LAST, lambda: None)

            count, more, upto, first, flag, base = (cnt[:, i, :] for i in range(6))
            dve.wait_ge(count_done, TILES + 1)
            own.did(dve.tensor_copy(count, C[0:1, 0:E]))
            own.did(dve.memset(one_f[:], 1.0))
            own.wait()
            own.did(dve.tensor_reduce(top[:, 0:1], count, AX.X, ALU.max))
            own.did(dve.tensor_scalar(more, count, CAP + 0.5, None, ALU.is_gt))
            own.did(dve.memset(top[:, 1:2], 1.0))
            own.wait()
            own.did(dve.tensor_scalar(tmp[0:1, 0, 0:1], top[:, 0:1], CAP + 0.5, None, ALU.is_gt))
            for r in range(2, ROUNDS):
                own.wait()
                own.did(dve.tensor_tensor(top[:, 1:2], top[:, 1:2], tmp[0:1, 0, 0:1], ALU.add))
                own.did(dve.tensor_scalar(flag, count, r * CAP + 0.5, None, ALU.is_gt))
                own.wait()
                own.did(dve.tensor_scalar(tmp[0:1, 0, 0:1], top[:, 0:1], r * CAP + 0.5, None, ALU.is_gt))
                own.did(dve.tensor_tensor(more, more, flag, ALU.add))
            own.wait()
            own.did(dve.tensor_tensor(top[:, 1:2], top[:, 1:2], tmp[0:1, 0, 0:1], ALU.add))
            own.did(dve.tensor_tensor_scan(upto, one_f[:, 0:E], more, 0.0, ALU.mult, ALU.add))
            own.wait()
            dve.tensor_copy(rounds[:], top[:, 1:2]).then_inc(rounds_known, 1)
            own.did(dve.tensor_tensor(first, upto, more, ALU.subtract))
            own.wait()
            own.did(dve.tensor_scalar(first, first, float(CAP), float(OVER_ROW - SPARE_ROW), ALU.mult, ALU.add))
            own.did(dve.tensor_scalar(y_row[:, 0:E], iota_e[0:1, :], float(CAP), None, ALU.mult))
            own.wait()
            for r in range(1, ROUNDS):
                own.did(dve.tensor_scalar(flag, more, r - 0.5, None, ALU.is_gt))
                own.did(dve.tensor_scalar(base, first, float((r - 1) * CAP), None, ALU.add))
                own.wait()
                own.did(dve.tensor_tensor(base, base, flag, ALU.mult))
                own.wait()
                own.did(dve.tensor_scalar(y_row[:, r * E:(r + 1) * E], base, float(SPARE_ROW), None, ALU.add))
                own.wait()
            own.did(dve.scalar_tensor_tensor(out=base, in0=iota_e[0:1, :], scalar=-float(CAP), in1=first,
                                             op0=ALU.mult, op1=ALU.add))
            own.wait()
            dve.tensor_scalar(base, base, float(SPARE_ROW - CAP), None, ALU.add).then_inc(shift_ready, 1)
            dve.wait_ge(count_done, TILES + 2)
            own.did(dve.tensor_copy(shift[:], C[:, 0:E]))

            row_of = tmp[:, 0, :]
            own.did(dve.scalar_tensor_tensor(out=row_of, in0=idx8[:].rearrange("p t k -> p (t k)"), scalar=float(CAP),
                                             in1=pos8[:].rearrange("p t k -> p (t k)"), op0=ALU.mult, op1=ALU.add))
            own.wait()
            own.did(dve.tensor_scalar(row_of, row_of, -1.0, None, ALU.add))
            own.clear()
            dve.wait_ge(rounds_known, 1)
            n_rounds = dve.value_load(rounds[0:1, 0:1], min_val=1, max_val=ROUNDS)
            with dve.If(n_rounds > 1):
                for t in range(TILES):
                    own.did(dve.tensor_tensor(
                        hot[:], iota_e[:].rearrange("p (a e) -> p a e", a=1).broadcast_to([P, TOP, E]),
                        idx8[:, t, :].rearrange("p (k e) -> p k e", e=1).broadcast_to([P, TOP, E]), ALU.is_equal))
                    own.wait()
                    hot_sum(shift[:], sel8[:])
                    own.did(dve.tensor_scalar(v8[:], pos8[:, t, :], CAP + 0.5, None, ALU.is_gt))
                    own.wait()
                    own.did(dve.tensor_tensor(sel8[:], sel8[:], v8[:], ALU.mult))
                    own.wait()
                    own.did(dve.tensor_tensor(row_of[:, t * TOP:(t + 1) * TOP], row_of[:, t * TOP:(t + 1) * TOP],
                                              sel8[:], ALU.add))
                own.clear()
            own.did(dve.tensor_tensor(
                tmp[:, 1, :].rearrange("p (t k) -> p t k", k=TOP), row_of.rearrange("p (t k) -> p t k", k=TOP),
                valid[:].rearrange("p (t k) -> p t k", k=1).broadcast_to([P, TILES, TOP]), ALU.mult))
            own.wait()
            own.did(dve.tensor_copy(slots[:], tmp[:, 1, :]))
            own.wait()



def experts(nc, a, c, keep, rows_dram, y_dram):
    ident, place, rounds, y_row = (keep[n] for n in ("ident", "place", "rounds", "y_row"))
    raw = dict(g=keep["raw_g"], u=keep["raw_u"], d=keep["raw_d"])
    ld = dict(g=keep["g_ld"], u=keep["u_ld"], d=keep["d_ld"])
    with ExitStack() as ctx:
        def sb(name, shape, dt=F32):
            return ctx.enter_context(nc.sbuf_tensor(name, shape, dt))

        def sem(name):
            return ctx.enter_context(nc.semaphore(name))

        hi = {m: sb(f"hi_{m}", list(raw[m].shape), F32R) for m in "gud"}
        lo = {m: sb(f"lo_{m}", list(raw[m].shape), F32R) for m in "gud"}
        x_hi = sb("x_hi", [P, KC, CAP], F32R)
        x_lo = sb("x_lo", [P, KC, CAP], F32R)
        h_hi = sb("h_hi", [P, FC, CAP], F32R)
        h_lo = sb("h_lo", [P, FC, CAP], F32R)
        rows = sb("rows", [P, 2, D])
        y = sb("y", [P, 2, D])
        sig = sb("sig", [P, FC, CAP])
        h1 = sb("h1", [P, FC, CAP])
        h2 = sb("h2", [P, FC, CAP])
        hot = sb("hot_slots", [P, TILES, 2 * P], BF16)
        iota1_f = sb("iota1_f", [P, CAP])
        iota1 = sb("iota1", [P, CAP], BF16)
        tok_f = sb("tok_f", [P, TILES, 2])
        tok = sb("tok", [P, TILES, 2], BF16)
        idx = sb("idx", [P, 2], I32)
        idx_f = sb("idx_f", [P, 2])
        warm = sb("warm", [1, 2])

        GU = [ctx.enter_context(nc.psum_tensor(f"GU{i}", [P, 512], F32)) for i in range(2)]
        T = [ctx.enter_context(nc.psum_tensor(f"T{i}", [P, 512], F32)) for i in range(4)]
        Y = [ctx.enter_context(nc.psum_tensor(f"Y{i}", [P, 512], F32)) for i in range(2)]
        L = T[3][:, 2 * CAP:2 * CAP + 4]

        hi_set = {m: sem(f"hi_set_{m}") for m in "gud"}
        lo_set = {m: sem(f"lo_set_{m}") for m in "gud"}
        consts, hot_ready, l_done, idx_ready, rows_ld, x_tr, x_hi_ev, x_lo_ev = (
            sem(n) for n in ("consts3", "hot_ready", "l_done", "idx_ready", "rows_ld", "x_tr3", "x_hi_ev", "x_lo_ev"))
        g_used, gu_done, sig_ready, h_ready, y_done, y_ev, y_st = (
            sem(n) for n in ("g_used", "gu_done", "sig_ready", "h_ready3", "y_done3", "y_ev", "y_st"))
        act_passed, warmed = sem("act_passed"), sem("warmed")
        dve_own, pool_on = sem("dve_own_experts"), sem("pool_on")
        NJ = E + 1
        HI_PARTS = dict(g=1, u=2, d=1)
        NL = E + 2
        NH = E + 3

        block = ctx.enter_context(nc.Block())

        def each_round(eng, body):
            n = eng.value_load(rounds[0:1, 0:1], min_val=1, max_val=ROUNDS)
            with eng.Fori(0, n) as r:
                body(r)

        @block.sync
        def _(sp):
            def load(e, m):
                for name, w in (("g", "w_exp_gate"), ("u", "w_exp_up"), ("d", "w_exp_down")):
                    src = a[w][0][bass.ds(e, 1)]
                    src = (src.rearrange("e (f p) d -> p (e f) d", p=P) if name == "d" else
                           src.rearrange("e (p k) f -> p (e k) f", k=KC))
                    sp.wait_ge(lo_set[name], m + 1)
                    sp.dma_start(raw[name][:], src).then_inc(ld[name], 16)

            sp.dma_start(iota1_f[:], c["iota1"]).then_inc(y_st, 16)
            sp.dma_start(tok_f[:], c["tok"]).then_inc(consts, 16)

            def one_round(r):
                with sp.Fori(0, E - 1) as n:
                    e = sp.snap(n + 1)
                    load(e, r * E + n)
                load(0, r * E + (E - 1))
            each_round(sp, one_round)

        @block.gpsimd
        def _(pool):
            pool.memset(hot[:, :, CAP:2 * P], 0.0).then_inc(pool_on, 1)
            pool.memset(warm[:], 0.0).then_inc(pool_on, 1)

            def one_round(r):
                with pool.Fori(0, NL) as k:
                    pool_after(pool, keep["passed"], idx_ready, r * NL + k + 2)
                    pool_after(pool, keep["passed"], x_tr, 4 * (r * NJ + k) + 1)
                    for b in range(2):
                        pool.indirect_dma_start(
                            out=rows[0:BLK[b], b, :], out_offset=None, in_=rows_dram[:, :],
                            in_offset=bass.IndirectOffsetOnAxis(ap=idx[0:BLK[b], b:b + 1], axis=0),
                        ).then_inc(rows_ld, 16)
                pool_after(pool, keep["passed"], rows_ld, 32 * NL * r + 32 * NL)
            each_round(pool, one_round)

        @block.tensor
        def _(pe):
            def three(out, lhs, rhs, first, last):
                for i, (x, w) in enumerate(((0, 0), (0, 1), (1, 0))):
                    ins = pe.matmul(out, lhs[x], rhs[w], start=first and i == 0, stop=last and i == 2)
                return ins

            def make_list(j, h, rows_read):
                pe.wait_ge(hot_ready, h + 1)
                pe.wait_ge(idx_ready, j + 1)
                pe.wait_ge(x_lo_ev, rows_read)
                for b in range(2):
                    for t in range(TILES):
                        ins = pe.matmul(L[:, 2 * b:2 * b + 2], hot[:, t, b * P:(b + 1) * P], tok[:, t, :],
                                        start=(t == 0), stop=(t == TILES - 1))
                ins.then_inc(l_done, 1)

            def transposes(j, gathered):
                pe.wait_ge(rows_ld, 32 * gathered)
                for i in range(4):
                    bank = T[i]
                    if i == 0:
                        pe.wait_ge(x_lo_ev, 4 * j + 1)
                    for k in range(2):
                        for b in range(2):
                            ins = pe.transpose(bank[:, k * CAP + b * P:k * CAP + b * P + BLK[b]],
                                               rows[0:BLK[b], b, (2 * i + k) * P:(2 * i + k + 1) * P],
                                               ident[0:BLK[b], 0:BLK[b]])
                    ins.then_inc(x_tr, 1)

            def gate_up(m):
                for mat, off in (("g", 0), ("u", CAP)):
                    pe.wait_ge(lo_set[mat], m + 1)
                    for f in range(FC):
                        for k in range(KC):
                            w = slice(f * P, (f + 1) * P)
                            ins = three(GU[f][:, off:off + CAP], (hi[mat][:, k, w], lo[mat][:, k, w]),
                                        (x_hi[:, k, :], x_lo[:, k, :]), k == 0, k == KC - 1)
                        if mat == "u":
                            ins.then_inc(gu_done, 1)
                    if mat == "g":
                        ins.then_inc(g_used, 1)

            def down(m):
                pe.wait_ge(lo_set["d"], m + 1)
                for q in range(4):
                    b, half = divmod(q, 2)
                    rows_b = slice(b * P, b * P + BLK[b])
                    cols = slice(half * 512, (half + 1) * 512)
                    pe.wait_ge(y_ev, 4 * m + q + 1)
                    for f in range(FC):
                        if q == 0:
                            pe.wait_ge(h_ready, 2 * m + f + 1)
                        ins = three(Y[half][0:BLK[b], :], (h_hi[:, f, rows_b], h_lo[:, f, rows_b]),
                                    (hi["d"][:, f, cols], lo["d"][:, f, cols]), f == 0, f == FC - 1)
                    ins.then_inc(y_done, 1)

            pe.wait_ge(consts, 16)
            pe.wait_ge(pool_on, 1)

            def one_round(r):
                make_list(r * NL, r * NH, 4 * r * NJ + 1)
                transposes(r * NJ, r * NL + 1)
                make_list(r * NL + 1, r * NH + 1, 4 * r * NJ + 5)
                with pe.Fori(0, E) as n:
                    pe.wait_ge(x_lo_ev, 4 * (r * NJ + n) + 5)
                    gate_up(r * E + n)
                    make_list(r * NL + n + 2, r * NH + n + 2, 4 * (r * NJ + n) + 5)
                    transposes(r * NJ + n + 1, r * NL + n + 2)
                    down(r * E + n)
            each_round(pe, one_round)

        @block.scalar
        def _(act):
            def split_hi(name, m, part=0):
                n = raw[name].shape[1] // HI_PARTS[name]
                w = slice(part * n, (part + 1) * n)
                ins = act.activation(hi[name][:, w, :], raw[name][:, w, :], ACT.Copy)
                ins.then_inc(hi_set[name], 1)

            def x_parts(j):
                for i in range(4):
                    act.wait_ge(x_tr, 4 * j + i + 2)
                    act.activation(x_hi[:, 2 * i:2 * i + 2, :], T[i][:, 0:2 * CAP].rearrange(
                        "p (k q) -> p k q", k=2), ACT.Copy).then_inc(x_hi_ev, 1)

            act.sem_inc(x_tr, 1)
            act.sem_inc(y_ev, 1)
            act.wait_ge(pool_on, 2)
            for name in "gud":
                act.wait_ge(ld[name], 16)
                for part in range(HI_PARTS[name]):
                    split_hi(name, 0, part)

            def copy_out(m, q):
                b, half = divmod(q, 2)
                act.wait_ge(y_done, 4 * m + q + 1)
                act.activation(y[0:BLK[b], b, half * 512:(half + 1) * 512], Y[half][0:BLK[b], :],
                               ACT.Copy).then_inc(y_ev, 1)

            def store(first, m, b):
                at = act.snap(first + b * P)
                act.wait_ge(y_ev, 4 * m + 2 * b + 4)
                act.dma_start(y_dram[bass.ds(at, BLK[b])], y[0:BLK[b], b, :]).then_inc(y_st, 16)

            def one_round(r):
                x_parts(r * NJ)
                with act.Fori(0, E) as n:
                    m = r * E + n
                    j = r * NJ + n + 1
                    first = act.value_load(y_row[0:1, bass.ds(m, 1)], min_val=0, max_val=SPARE_ROW)
                    act.activation(warm[:], warm[:], ACT.Sigmoid).then_inc(warmed, 1)
                    act.wait_ge(ld["g"], 16 * m + 32)
                    act.wait_ge(g_used, m + 1)
                    split_hi("g", m + 1)
                    for f in range(FC):
                        act.wait_ge(gu_done, 2 * m + f + 1)
                        act.activation(sig[:, f, :], GU[f][:, 0:CAP], ACT.Sigmoid).then_inc(sig_ready, 1)
                    x_parts(j)
                    act.wait_ge(ld["u"], 16 * m + 32)
                    split_hi("u", m + 1, 0)
                    act.wait_ge(y_st, 32 * m + 16)
                    copy_out(m, 0)
                    split_hi("u", m + 1, 1)
                    copy_out(m, 1)
                    store(first, m, 0)
                    copy_out(m, 2)
                    copy_out(m, 3)
                    store(first, m, 1)
                    act.wait_ge(ld["d"], 16 * m + 32)
                    split_hi("d", m + 1)
                act.wait_ge(y_st, 32 * E * r + 32 * E + 16)
                act.sem_inc(act_passed, 1)
            each_round(act, one_round)

        @block.vector
        def _(dve):
            own = Chain(dve, dve_own)

            def split_lo(name, m):
                dve.wait_ge(hi_set[name], HI_PARTS[name] * (m + 1))
                dve.tensor_tensor(lo[name][:], raw[name][:], hi[name][:].bitcast(F32),
                                  ALU.subtract).then_inc(lo_set[name], 1)

            def one_hot(j, e):
                dve.wait_ge(l_done, j + 1)
                dve.tensor_tensor(hot[:, :, 0:CAP],
                                  iota1[:].rearrange("p (a s) -> p a s", a=1).broadcast_to([P, TILES, CAP]),
                                  place[:, e, :].rearrange("p (t a) -> p t a", a=1).broadcast_to([P, TILES, CAP])
                                  if isinstance(e, int) else
                                  place[:, bass.ds(e, 1), :].rearrange("p a t -> p t a").broadcast_to(
                                      [P, TILES, CAP]),
                                  ALU.is_equal).then_inc(hot_ready, 1)

            def to_index(j):
                dve.wait_ge(l_done, j + 2)
                own.did(dve.tensor_reduce(idx_f[:], L.rearrange("p (b a) -> p b a", a=2), AX.X, ALU.add))
                own.wait()
                dve.tensor_copy(idx[:], idx_f[:]).then_inc(idx_ready, 1)

            def x_parts(j):
                for i in range(4):
                    w = slice(2 * i, 2 * i + 2)
                    dve.wait_ge(x_hi_ev, 4 * j + i + 1)
                    dve.tensor_tensor(x_lo[:, w, :], T[i][:, 0:2 * CAP].rearrange("p (k q) -> p k q", k=2),
                                      x_hi[:, w, :].bitcast(F32), ALU.subtract).then_inc(x_lo_ev, 1)

            def hidden(m, f):
                dve.wait_ge(sig_ready, 2 * m + f + 1)
                own.did(dve.tensor_tensor(h1[:, f, :], sig[:, f, :], GU[f][:, 0:CAP], ALU.mult))
                own.wait()
                own.did(dve.tensor_tensor(h2[:, f, :], h1[:, f, :], GU[f][:, CAP:2 * CAP], ALU.mult))
                own.wait()
                own.did(dve.tensor_copy(h_hi[:, f, :], h2[:, f, :]))
                own.wait()
                dve.tensor_tensor(h_lo[:, f, :], h2[:, f, :], h_hi[:, f, :].bitcast(F32),
                                  ALU.subtract).then_inc(h_ready, 1)

            dve.sem_inc(l_done, 1)
            dve.sem_inc(idx_ready, 1)
            dve.sem_inc(x_lo_ev, 1)
            dve.sem_inc(y_ev, 1)
            dve.wait_ge(consts, 16)
            dve.wait_ge(y_st, 16)
            own.did(dve.tensor_copy(iota1[:], iota1_f[:]))
            own.did(dve.tensor_copy(tok[:], tok_f[:]))
            own.clear()
            for name in "gud":
                split_lo(name, 0)

            def one_round(r):
                one_hot(r * NL, 0)
                to_index(r * NL)
                one_hot(r * NL + 1, 1)
                x_parts(r * NJ)
                to_index(r * NL + 1)
                one_hot(r * NL + 2, 2)
                own.clear()
                with dve.Fori(0, E) as n:
                    m = r * E + n
                    following = dve.snap(n + 3)
                    split_lo("g", m + 1)
                    hidden(m, 0)
                    hidden(m, 1)
                    x_parts(r * NJ + n + 1)
                    split_lo("u", m + 1)
                    to_index(r * NL + n + 2)
                    one_hot(r * NL + n + 3, following)
                    split_lo("d", m + 1)
                    own.clear()
                dve.wait_ge(hot_ready, NH * r + NH)
                dve.wait_ge(rows_ld, 32 * NL * r + 32 * NL)
                own.did(dve.tensor_scalar(place[:], place[:], -float(CAP), None, ALU.add))
                own.clear()
            each_round(dve, one_round)



def output(nc, a, o, keep, y_dram):
    resid, ident, w8, slots = (keep[n] for n in ("resid", "ident", "w8", "slots"))
    LAST = TILES - 1
    with ExitStack() as ctx:
        def sb(name, shape, dt=F32):
            return ctx.enter_context(nc.sbuf_tensor(name, shape, dt))

        def sem(name):
            return ctx.enter_context(nc.semaphore(name))

        w_gate = sb("w_gate", [P, KC, D])
        w_proj = sb("w_proj", [P, PLE // P, D])
        ple = sb("ple", [P, TILES, PLE])
        g_ple = sb("g_ple", [P, D])
        g_fin = sb("g_fin", [P, D])
        yk = sb("yk", [P, TOP, D])
        idx = sb("idx_k", [P, TOP], I32)
        wk = sb("wk", [P, TOP])
        ple_t = sb("ple_t", [P, PLE])
        row = sb("row4", [P, D])
        colT = sb("colT4", [P, KC, P])
        pT = sb("pT", [P, PLE // P, P])
        gate = sb("gate", [P, D])
        inj = sb("inj", [P, D])
        out = sb("out", [P, D])
        junk = sb("junk4", [P, D], BF16)
        st = sb("st4", [P, 8])
        half = sb("half4", [P, 1])

        X = [ctx.enter_context(nc.psum_tensor(f"OX{i}", [P, 512], F32)) for i in range(2)]
        XP = ctx.enter_context(nc.psum_tensor("OXP", [P, 512], F32))
        J = [ctx.enter_context(nc.psum_tensor(f"OJ{i}", [P, 512], F32)) for i in range(2)]
        G = [ctx.enter_context(nc.psum_tensor(f"OG{i}", [P, 512], F32)) for i in range(2)]

        w_ld, zeroed, idx_ready, wk_ready, added, sumsq, row_ready, x_tr, x_ev = (
            sem(n) for n in ("w_ld4", "zeroed4", "idx_ready4", "wk_ready", "added4", "sumsq4", "row_ready4", "x_tr4",
                             "x_ev4"))
        p_ready, p_tr, p_ev, j_done, g_done, g_ready, injected, fin_sq, out_ready, out_st = (
            sem(n) for n in ("p_ready4", "p_tr", "p_ev", "j_done", "g_done4", "g_ready", "injected", "fin_sq",
                             "out_ready", "out_st"))
        y_ld = [sem(f"y_ld{k}") for k in range(TOP)]
        dve_own = sem("dve_own_output")
        pool_own, rstd_ready, fin_ready = sem("pool_own_output"), sem("rstd_ready4"), sem("fin_ready")

        block = ctx.enter_context(nc.Block())

        @block.sync
        def _(sp):
            sp.dma_start(g_ple[:], a["g_ple"][0:1, :].broadcast_to([P, D])).then_inc(w_ld, 16)
            sp.dma_start(ple[:, 0:PROMPT_TILES, :], a["p_prompt"][0, 0].rearrange("(t p) d -> p t d", p=P)).then_inc(
                w_ld, 16)
            sp.dma_start(ple[0:NS, SAMPLE, :], a["p_sample"][0].rearrange("b s d -> (b s) d")).then_inc(w_ld, 16)
            sp.dma_start(w_proj[:], a["w_ple_proj"][0].rearrange("(f p) d -> p f d", p=P)).then_inc(w_ld, 16)
            sp.dma_start(w_gate[:], a["w_ple_gate"][0].rearrange("(p k) n -> p k n", k=KC)).then_inc(w_ld, 16)
            sp.dma_start(g_fin[:], a["g_final"].rearrange("(a d) -> a d", a=1).broadcast_to([P, D])).then_inc(w_ld, 16)
            with sp.Fori(0, PROMPT_TILES) as t:
                at = sp.snap(t * P)
                sp.wait_ge(out_ready, t + 1)
                sp.dma_start(o["y_prompt"][0][bass.ds(at, P)], out[:]).then_inc(out_st, 16)
            sp.wait_ge(out_ready, TILES)
            sp.dma_start(o["y_sample"].rearrange("b s d -> (b s) d"), out[0:NS, :]).then_inc(out_st, 16)
            sp.wait_ge(out_st, 16 * TILES)

        @block.gpsimd
        def _(pool):
            pool.memset(ple[NS:P, SAMPLE, :], 0.0).then_inc(zeroed, 1)
            pool.wait_ge(zeroed, 1)

            n_rounds = pool.value_load(keep["rounds"][0:1, 0:1], min_val=1, max_val=ROUNDS)

            def tile(t):
                pool_after(pool, keep["passed"], added, TOP * t)
                pool.tensor_copy(idx[:], slots[:, bass.ds(t * TOP, TOP)]).then_inc(idx_ready, 1)
                pool.tensor_copy(wk[:], w8[:, t, :]).then_inc(wk_ready, 1)
                pool_after(pool, keep["passed"], idx_ready, t + 1)
                for several, table in ((n_rounds < 2, y_dram[0:OVER_ROW, :]), (n_rounds > 1, y_dram[:, :])):
                    with pool.If(several):
                        for k in range(TOP):
                            pool.indirect_dma_start(
                                out=yk[:, k, :], out_offset=None, in_=table,
                                in_offset=bass.IndirectOffsetOnAxis(ap=idx[:, k:k + 1], axis=0)).then_inc(y_ld[k], 16)
                pool_after(pool, keep["passed"], p_tr, t)
                pool.tensor_copy(ple_t[:], ple[:, t, :]).then_inc(p_ready, 1)

            pool.memset(half[:], -0.5).then_inc(zeroed, 1)
            pool.wait_ge(zeroed, 2)
            pool.wait_ge(w_ld, 16 * 6)
            own = Chain(pool, pool_own)

            def norm_in(t):
                pool_after(pool, keep["passed"], sumsq, t + 1)
                rstd(own, pool, st[:, 1:2], st[:, 0:1], D, half[:], rstd_ready)

            def norm_out(t):
                pool_after(pool, keep["passed"], fin_sq, t + 1)
                rstd(own, pool, st[:, 5:6], st[:, 4:5], D, half[:], fin_ready)
                own.clear()

            tile(0)
            norm_in(0)
            own.clear()
            with pool.Fori(0, LAST) as t:
                tile(t + 1)
                norm_in(t + 1)
                norm_out(t)
            norm_out(LAST)

        @block.tensor
        def _(pe):
            def tile(t):
                pe.wait_ge(p_ready, t + 1)
                after(pe, p_ev, t)
                for f in range(PLE // P):
                    ins = pe.transpose(XP[:, f * P:(f + 1) * P], ple_t[:, f * P:(f + 1) * P], ident[:])
                ins.then_inc(p_tr, 1)
                pe.wait_ge(row_ready, t + 1)
                after(pe, x_ev, 2 * t)
                for b in range(2):
                    for k in range(4):
                        ins = pe.transpose(X[b][:, k * P:(k + 1) * P], row[:, (4 * b + k) * P:(4 * b + k + 1) * P],
                                           ident[:])
                    ins.then_inc(x_tr, 1)
                pe.wait_ge(p_ev, t + 1)
                after(pe, injected, 2 * t)
                for half in range(2):
                    for f in range(PLE // P):
                        ins = pe.matmul(J[half][:], pT[:, f, :], w_proj[:, f, half * 512:(half + 1) * 512],
                                        start=(f == 0), stop=(f == PLE // P - 1))
                    ins.then_inc(j_done, 1)
                pe.wait_ge(x_ev, 2 * t + 2)
                after(pe, g_ready, 2 * t)
                for half in range(2):
                    for k in range(KC):
                        ins = pe.matmul(G[half][:], colT[:, k, :], w_gate[:, k, half * 512:(half + 1) * 512],
                                        start=(k == 0), stop=(k == KC - 1))
                    ins.then_inc(g_done, 1)

            pe.wait_ge(w_ld, 16 * 6)
            tile(0)
            with pe.Fori(1, TILES) as t:
                tile(t)

        @block.scalar
        def _(act):
            def square_sum(t):
                act.wait_ge(added, TOP * t + TOP)
                act.activation(junk[:], resid[:, t, :], ACT.Square, accum_out=st[:, 0:1]).then_inc(sumsq, 1)

            def tile(t, then):
                act.wait_ge(p_tr, t + 1)
                act.activation(pT[:].rearrange("p f q -> p (f q)"), XP[:, 0:PLE], ACT.Copy).then_inc(p_ev, 1)
                act.wait_ge(x_tr, 2 * t + 1)
                act.activation(colT[:, 0:4, :], X[0][:].rearrange("p (k q) -> p k q", k=4),
                               ACT.Copy).then_inc(x_ev, 1)
                then()
                for half in range(2):
                    act.wait_ge(g_done, 2 * t + half + 1)
                    act.activation(gate[:, half * 512:(half + 1) * 512], G[half][:], ACT.Sigmoid).then_inc(g_ready, 1)
                act.wait_ge(injected, 2 * t + 2)
                act.activation(junk[:], resid[:, t, :], ACT.Square, accum_out=st[:, 4:5]).then_inc(fin_sq, 1)

            square_sum(0)
            tile(0, lambda: square_sum(1))
            with act.Fori(1, LAST) as t:
                tile(t, lambda: square_sum(t + 1))
            tile(LAST, lambda: None)

        @block.vector
        def _(dve):
            own = Chain(dve, dve_own)

            def gather_sum(t):
                dve.wait_ge(wk_ready, t + 1)
                for k in range(TOP):
                    dve.wait_ge(y_ld[k], 16 * (t + 1))
                    if k:
                        dve.wait_ge(added, TOP * t + k)
                    dve.scalar_tensor_tensor(out=resid[:, t, :], in0=yk[:, k, :], scalar=wk[:, k:k + 1],
                                             in1=resid[:, t, :], op0=ALU.mult, op1=ALU.add).then_inc(added, 1)

            def norm(t):
                dve.wait_ge(rstd_ready, t + 1)
                dve.scalar_tensor_tensor(out=row[:].rearrange("p (k q) -> p q k", k=KC),
                                         in0=resid[:, t, :].rearrange("p (q k) -> p q k", k=KC), scalar=st[:, 1:2],
                                         in1=g_ple[:].rearrange("p (q k) -> p q k", k=KC),
                                         op0=ALU.mult, op1=ALU.mult).then_inc(row_ready, 1)

            def tile(t, then):
                dve.wait_ge(x_tr, 2 * t + 2)
                dve.tensor_copy(colT[:, 4:8, :], X[1][:].rearrange("p (k q) -> p k q", k=4)).then_inc(x_ev, 1)
                then()
                for half in range(2):
                    w = slice(half * 512, (half + 1) * 512)
                    dve.wait_ge(g_ready, 2 * t + half + 1)
                    dve.wait_ge(j_done, 2 * t + half + 1)
                    own.did(dve.tensor_tensor(inj[:, w], gate[:, w], J[half][:], ALU.mult))
                    own.wait()
                    dve.tensor_tensor(resid[:, t, w], resid[:, t, w], inj[:, w], ALU.add).then_inc(injected, 1)
                dve.wait_ge(fin_ready, t + 1)
                after(dve, out_st, 16 * t)
                dve.scalar_tensor_tensor(out=out[:], in0=resid[:, t, :], scalar=st[:, 5:6], in1=g_fin[:],
                                         op0=ALU.mult, op1=ALU.mult).then_inc(out_ready, 1)
                own.clear()

            dve.wait_ge(w_ld, 16 * 6)
            dve.wait_ge(zeroed, 1)
            gather_sum(0)
            norm(0)

            def following(t):
                gather_sum(t + 1)
                norm(t + 1)
            tile(0, lambda: following(0))
            with dve.Fori(1, LAST) as t:
                tile(t, lambda: following(t))
            tile(LAST, lambda: None)



def constants():
    c = {}
    f = np.float32
    inv = np.power(f(THETA), -np.arange(HALF, dtype=f) * f(2.0) / f(2 * HALF)).astype(f)
    pos = np.zeros((TILES, P), f)
    pos[:PROMPT_TILES] = np.arange(SEQ).reshape(PROMPT_TILES, P)
    pos[SAMPLE, :NS] = PAST + np.arange(NS) % STEPS
    ang = (pos[:, :, None] * inv[None, None, :]).astype(f)
    c["rope"] = np.stack([np.cos(ang), np.sin(ang)], axis=2).transpose(1, 0, 2, 3).astype(f)
    q, k = np.arange(P)[:, None], np.arange(2 * P)[None, :]
    later = (k >= q) & (k <= q + P)
    c["amask"] = np.where(np.stack([later & (k >= P), later], axis=1), f(0), f(NEG)).astype(f)
    rows = np.arange(P)
    i, s = rows // 32, rows % STEPS
    sm = np.full((P, 2, P + NS), NEG, f)
    for h in range(2):
        sm[:, h, :P][np.arange(P)[None, :] >= s[:, None]] = 0
        kb, ks = np.arange(NS) // STEPS, np.arange(NS) % STEPS
        sm[:, h, P:][(kb[None, :] == (4 * h + i)[:, None]) & (ks[None, :] <= s[:, None])] = 0
    c["smask"] = sm
    pick = np.zeros((P, KV_HEADS, HEADS), f)
    for g in range(KV_HEADS):
        pick[rows, g, GROUP * g + (rows % 32) // STEPS] = 1
    c["pick"] = pick
    pm = np.zeros((P, 3, PG, P), f)
    src, dst = np.arange(P)[:, None], np.arange(P)[None, :]
    for g, w in enumerate(POOL_WINDOWS):
        inside = (src <= dst) & (src > dst - w)
        pm[:, 0, g] = inside / np.minimum(dst + 1, w) - (src == dst)
        pm[:, 1, g] = inside / w - (src == dst)
        pm[:, 2, g] = (src - P > dst - w) / w
    c["pmat"] = pm.astype(f)
    ps = np.zeros((P, 2, PG, NS), f)
    db, ds_ = np.arange(NS) // STEPS, np.arange(NS) % STEPS
    nb, nstep = np.arange(NS) // STEPS, np.arange(NS) % STEPS
    sb_, sr = np.arange(SEQS * PREFIX) // PREFIX, np.arange(SEQS * PREFIX) % PREFIX - PREFIX
    for g, w in enumerate(POOL_WINDOWS):
        same = nb[:, None] == db[None, :]
        ps[:NS, 0, g] = (same & (nstep[:, None] <= ds_) & (nstep[:, None] > ds_ - w)) / w - np.eye(NS)
        ps[:SEQS * PREFIX, 1, g] = ((sb_[:, None] == db[None, :]) & (sr[:, None] > ds_ - w)) / w
    c["pmat_s"] = ps.astype(f)
    c["tri"] = (src < dst).astype(f)
    c["iota_e"] = np.broadcast_to(np.arange(E, dtype=f), (P, E)).copy()
    v = np.ones((P, TILES), f)
    v[NS:, SAMPLE] = 0
    c["valid"] = v
    c["iota1"] = np.broadcast_to(np.arange(1, CAP + 1), (P, CAP)).astype(f)
    tok = np.zeros((P, TILES, 2))
    tok[:, :, 0] = np.arange(P)[:, None]
    tok[:, :, 1] = P * np.arange(TILES)[None, :]
    c["tok"] = tok.astype(f)
    return c


OUTS = {
    "y_prompt": (1, SEQ, D), "y_sample": (SEQS, STEPS, D),
    "k_prompt": (1, 1, WINDOW, KV_HEADS, HD), "v_prompt": (1, 1, WINDOW, KV_HEADS, HD),
    "pool_prompt": (1, 1, PREFIX, POOL),
    "k_sample": (1, SEQS, WINDOW, KV_HEADS, HD), "v_sample": (1, SEQS, WINDOW, KV_HEADS, HD),
    "pool_sample": (1, SEQS, PREFIX, POOL),
}


def kernel(**inputs):
    import concourse.bacc as bacc
    from concourse.bass_utils import run_bass_kernel_spmd as run

    nc = bacc.Bacc("TRN2", target_bir_lowering=False, num_devices=1)
    arrays = {}

    def declare(prefix, named):
        aps = {}
        for name, x in named.items():
            x = np.ascontiguousarray(x)
            arrays[f"{prefix}_{name}"] = x
            aps[name] = nc.dram_tensor(f"{prefix}_{name}", x.shape, mybir.dt.from_np(x.dtype),
                                       kind="ExternalInput").ap()
        return aps

    a = declare("in", inputs)
    c = declare("const", constants())
    o = {name: nc.dram_tensor(f"out_{name}", shape, F32, kind="ExternalOutput").ap() for name, shape in OUTS.items()}
    build(nc, a, o, c)
    r = run(nc, [arrays], core_ids=[0]).results[0]
    return tuple(r[f"out_{name}"] for name in OUTS)
```

```python
from contextlib import ExitStack

import numpy as np
import concourse.bass as bass
from concourse import mybir

F32 = mybir.dt.float32
F32R = mybir.dt.float32r
BF16 = mybir.dt.bfloat16
I32 = mybir.dt.int32
U32 = mybir.dt.uint32
ALU = mybir.AluOpType
ACT = mybir.ActivationFunctionType
AX = mybir.AxisListType

P = 128
D = 1024
SEQ = 1024
PROMPT_TILES = SEQ // P
SEQS = 8
STEPS = 8
NS = SEQS * STEPS
TILES = PROMPT_TILES + 1
SAMPLE = PROMPT_TILES
LAST_PROMPT = PROMPT_TILES - 1
PAST = 8192
HEADS, KV_HEADS, HD = 8, 2, 64
GROUP = HEADS // KV_HEADS
ATT = HEADS * HD
KV = KV_HEADS * HD
POOL = D - ATT
IN_W = ATT + 2 * KV + POOL
K0, V0, U0 = ATT, ATT + KV, ATT + 2 * KV
WINDOW = 128
HALF = HD // 8
THETA = 500000.0
POOL_WINDOWS = (2, 4, 8, 16)
PG = len(POOL_WINDOWS)
PREFIX = 15
KC = D // P
E = 64
EG = 8
TOP = 8
TOP_GROUPS = 4
FE = 256
FC = FE // P
ROUTED_SCALE = 2.5
PLE = 256
EPS = 1e-6
SCALE = HD ** -0.5
NEG = -1e30
CAP = 212
ROUNDS = -(-(SEQ + NS) // CAP)
BLK = (P, CAP - P)
OVER_ROW = E * CAP
SPARE_ROW = OVER_ROW + (SEQ + NS) * TOP
Y_ROWS = SPARE_ROW + CAP


def after(eng, sem, value):
    if not (isinstance(value, int) and value <= 0):
        eng.wait_ge(sem, value)


def pool_after(pool, passed, sem, value):
    after(pool, sem, value)
    pool.sem_inc(passed, 1)


class Chain:

    def __init__(self, eng, sem):
        self.eng, self.sem, self.n = eng, sem, 0

    def did(self, ins):
        ins.then_inc(self.sem, 1)
        self.n += 1

    def wait(self):
        self.eng.wait_ge(self.sem, self.n)

    def clear(self):
        self.wait()
        self.eng.sem_clear(self.sem)
        self.n = 0


def rstd(own, pool, dst, src, width, half, ready):
    own.did(pool.tensor_scalar(dst, src, 1.0 / width, EPS, ALU.mult, ALU.add))
    own.wait()
    pool.tensor_tensor(dst, dst, half, ALU.pow).then_inc(ready, 1)


def build(nc, a, o, c):
    rows_dram = nc.dram_tensor("rows_dram", (TILES * P, D), F32, kind="Internal").ap()
    y_dram = nc.dram_tensor("y_dram", (Y_ROWS, D), F32, kind="Internal").ap()
    o_dram = nc.dram_tensor("o_dram", (4, P, HD), F32, kind="Internal").ap()

    with ExitStack() as ctx:
        def sb(name, shape, dt=F32):
            return ctx.enter_context(nc.sbuf_tensor(name, shape, dt))
        keep = dict(
            resid=sb("resid", [P, TILES, D]),
            ident=sb("ident", [P, P]),
            w_big=sb("w_big", [P, KC * IN_W]),
            raw_g=sb("raw_g", [P, KC, FE]), raw_u=sb("raw_u", [P, KC, FE]), raw_d=sb("raw_d", [P, FC, D]),
            place=sb("place", [P, E + 3, TILES]),
            **{n: ctx.enter_context(nc.semaphore(n)) for n in ("g_ld", "u_ld", "d_ld", "router_ld", "output_ld", "passed")},
        )
        mixer(nc, a, o, c, keep, o_dram)
        keep |= dict(
            w8=sb("w8", [P, TILES, TOP]),
            slots=sb("slots", [P, TILES * TOP], I32),
            rounds=sb("rounds", [1, 1], I32),
            y_row=sb("y_row", [1, ROUNDS * E], I32),
            fill=sb("fill", [1, ROUNDS * E], I32),
            iota1=sb("iota1", [P, CAP], BF16), tok=sb("tok", [P, TILES, 2], BF16),
            ple=sb("ple", [P, TILES, PLE]),
        )
        with ExitStack() as split:
            for m in "gud":
                for part in ("hi", "lo"):
                    name = f"{part}_{m}"
                    keep[name] = split.enter_context(nc.sbuf_tensor(name, keep[f"raw_{m}"].shape, F32R))
                    keep[f"{part}_set_{m}"] = ctx.enter_context(nc.semaphore(f"{part}_set_{m}"))
            router(nc, a, c, keep, rows_dram, y_dram)
            experts(nc, a, c, keep, rows_dram, y_dram)
        output(nc, a, o, keep, y_dram)


def router_weights(a, c, keep):
    parts = (("s_gate", KC * FE, a["w_sh_gate"][0].rearrange("(p k) f -> p k f", k=KC), dict(k=KC)),
             ("s_up", KC * FE, a["w_sh_up"][0].rearrange("(p k) f -> p k f", k=KC), dict(k=KC)),
             ("s_down", FC * D, a["w_sh_down"][0].rearrange("(f p) d -> p f d", p=P), dict(k=FC)),
             ("g_ffn", D, a["g_ffn"][0:1, :].broadcast_to([P, D]), None),
             ("w_r", KC * E, a["w_router"][0].rearrange("(p k) e -> p k e", k=KC), dict(k=KC)),
             ("bias", E, a["router_bias"][0:1, :].broadcast_to([P, E]), None),
             ("iota_e", E, c["iota_e"], None), ("tri_f", P, c["tri"], None), ("valid", TILES, c["valid"], None))
    at, views = 0, {}
    for name, n, src, split in parts:
        place = keep["w_big"][:, at:at + n]
        views[name] = (place.rearrange("p (k f) -> p k f", **split) if split else place, src)
        at += n
    return views


HI_PARTS = dict(g=1, u=2, d=1)


def split_hi(act, keep, name, m, part):
    raw, hi = keep[f"raw_{name}"], keep[f"hi_{name}"]
    n = raw.shape[1] // HI_PARTS[name]
    w = slice(part * n, (part + 1) * n)
    act.activation(hi[:, w, :], raw[:, w, :], ACT.Copy).then_inc(keep[f"hi_set_{name}"], 1)


def split_lo(dve, keep, name, m):
    raw, hi, lo = keep[f"raw_{name}"], keep[f"hi_{name}"], keep[f"lo_{name}"]
    dve.wait_ge(keep[f"hi_set_{name}"], HI_PARTS[name] * (m + 1))
    dve.tensor_tensor(lo[:], raw[:], hi[:].bitcast(F32), ALU.subtract).then_inc(keep[f"lo_set_{name}"], 1)



def mixer(nc, a, o, c, keep, o_dram):
    resid, ident = keep["resid"], keep["ident"]
    with ExitStack() as ctx:
        def sb(name, shape, dt=F32):
            return ctx.enter_context(nc.sbuf_tensor(name, shape, dt))

        def sem(name):
            return ctx.enter_context(nc.semaphore(name))

        w_in = keep["w_big"][:].rearrange("p (k n) -> p k n", k=KC)
        w_out = sb("w_out", [P, KC, D])
        w_pool = sb("w_pool", [P, PG, P])
        g_mix = sb("g_mix", [P, D])
        g_mid = sb("g_mid", [P, D])
        p_scale = sb("p_scale", [P, POOL])
        sink = sb("sink", [P, HEADS])
        sink_s = sb("sink_s", [P, KV_HEADS])
        pick = sb("pick", [P, KV_HEADS, HEADS])
        picked = sb("picked", [P, KV_HEADS, HEADS])
        rope = sb("rope", [P, TILES, 2, HALF])
        amask = sb("amask", [P, 2, 2 * P])
        smask = sb("smask", [P, 2, P + NS])
        pmat = sb("pmat", [P, 3, PG, P])
        row = sb("row", [P, D])
        colT = sb("colT", [P, KC, P])
        colM = sb("colM", [P, KC, P])
        z = sb("z", [P, IN_W])
        rt = sb("rt", [P, 4, HEADS + KV_HEADS, HALF])
        qT = sb("qT", [P, GROUP, P])
        kT = sb("kT", [P, 2 * P])
        v_prev = sb("v_prev", [P, KV])
        u_prev = sb("u_prev", [P, POOL])
        prob = sb("prob", [P, HEADS, 2 * P])
        probT = sb("probT", [P, HEADS, 2, P])
        dT = sb("dT", [P, PG, P])
        mix = sb("mix", [P, D])
        junk = sb("junk", [P, D], BF16)
        st = sb("st", [P, 8])
        half = sb("half", [P, 2])
        mx = sb("mx", [P, HEADS])
        m8 = sb("m8", [P, 3, HEADS])
        den = sb("den", [P, HEADS])
        rden = sb("rden", [P, HEADS])
        late = keep["raw_d"][:].rearrange("p f d -> p (f d)")
        vc = late[:, 0:SEQS * KV].rearrange("p (b k) -> p b k", b=SEQS)
        ustate = late[0:SEQS * PREFIX, 1024:1024 + POOL]
        pmat_s = late[:, 1536:2048].rearrange("p (a g q) -> p a g q", a=2, g=PG)
        o_s = keep["place"][:].rearrange("p e t -> p (e t)")[:, 0:4 * HD].rearrange("p (c d) -> p c d", c=4)
        kc = probT[:].rearrange("p h b q -> p (h b q)")[:, 0:SEQS * KV].rearrange("p (b k) -> p b k", b=SEQS)
        kcT = probT[:].rearrange("p h b q -> p (h b q)")[:, SEQS * KV:2 * SEQS * KV].rearrange(
            "p (b k) -> p b k", b=SEQS)
        prob_s = prob[:].rearrange("p h k -> p (h k)")[:, 0:4 * (P + NS)].rearrange("p (c k) -> p c k", c=4)
        ptc = prob[:].rearrange("p h k -> p (h k)")[:, 1024:1024 + 4 * P].rearrange("p (c k) -> p c k", c=4)
        ptn = prob[:].rearrange("p h k -> p (h k)")[:, 1536:1536 + 4 * P].rearrange("p (c k) -> p c k", c=4)

        X = [ctx.enter_context(nc.psum_tensor(f"X{i}", [P, 512], F32)) for i in range(2)]
        Z = [ctx.enter_context(nc.psum_tensor(f"Z{i}", [P, 512], F32)) for i in range(2)]
        S = [ctx.enter_context(nc.psum_tensor(f"S{i}", [P, 512], F32)) for i in range(4)]

        x0_ld, x1_ld, g_mix_ld, x_ld, wout_ld, c_ld, late_ld, cache_ld = (sem(n) for n in (
            "x0_ld", "x1_ld", "g_mix_ld", "x_ld", "wout_ld", "c_ld", "late_ld", "cache_ld"))
        win_ld = [sem(f"win_ld{i}") for i in range(3)]
        ident_set, zeroed, sumsq, xs_ready, x_tr, x_ev, z_done, zk_ev = (sem(n) for n in (
            "ident_set", "zeroed", "sumsq", "xs_ready", "x_tr", "x_ev", "z_done", "zk_ev"))
        roped, d_done, dT_ev, qk_tr, qk_ev, s_done, y_done, m_ready, p_ready = (sem(n) for n in (
            "roped", "d_done", "dT_ev", "qk_tr", "qk_ev", "s_done", "y_done", "m_ready", "p_ready"))
        pt_tr, pt_dve, pt_act, o_done, prev_copied, mix_raw, mix_sq, mixed, m_tr, m_ev = (
            sem(n) for n in ("pt_tr", "pt_dve", "pt_act", "o_done", "prev_copied", "mix_raw", "mix_sq", "mixed",
                             "m_tr", "m_ev"))
        proj_done, added = ([sem(f"{n}{half}") for half in range(2)] for n in ("proj_done", "added"))
        kv_out, kc_tr, kc_ev, pts_ev, os_ready, o_st, o_back, copied = (sem(n) for n in (
            "kv_out", "kc_tr", "kc_ev", "pts_ev", "os_ready", "o_st", "o_back", "copied"))
        dve_own, pool_own, x_rstd, m_rstd = sem("dve_own_mixer"), sem("pool_own_mixer"), sem("x_rstd"), sem("m_rstd")

        NCONST = 8
        Z_IN = ((S[1], 0, 512), (S[2], 512, 1024), (S[3], 1024, IN_W))

        by_seq = o_dram.rearrange("(h g) (i j s) d -> h i g s j d", g=KV_HEADS, i=4, s=STEPS)

        def rows_back(queue, seqs):
            for b in seqs:
                for g in range(KV_HEADS):
                    dst = mix[b * STEPS:(b + 1) * STEPS, g * GROUP * HD:(g + 1) * GROUP * HD]
                    queue.dma_start(dst.rearrange("s (j d) -> s j d", d=HD), by_seq[b // 4, b % 4, g]).then_inc(o_back, 16)

        block = ctx.enter_context(nc.Block())

        @block.sync
        def _(sp):
            sp.dma_start(resid[:, 0, :], a["x_prompt"][0, 0:P, :]).then_inc(x0_ld, 16)
            sp.dma_start(g_mix[:], a["g_mix"][0:1, :].broadcast_to([P, D])).then_inc(g_mix_ld, 16)
            for i, (_, n0, n1) in enumerate(Z_IN):
                sp.dma_start(w_in[:, :, n0:n1], a["w_in"][0].rearrange("(p k) n -> p k n", k=KC)[:, :, n0:n1]).then_inc(
                    win_ld[i], 16)
                if i == 0:
                    sp.dma_start(rope[:], c["rope"]).then_inc(c_ld, 16)
            sp.dma_start(amask[:], c["amask"]).then_inc(c_ld, 16)
            sp.dma_start(pmat[:], c["pmat"]).then_inc(c_ld, 16)
            sp.dma_start(w_pool[:], a["w_pool"][0].rearrange("g c d -> c g d")).then_inc(c_ld, 16)
            sp.dma_start(p_scale[:], a["pool_scale"][0:1, :].broadcast_to([P, POOL])).then_inc(c_ld, 16)
            sp.dma_start(sink[:], a["attn_sinks"][0:1, :].broadcast_to([P, HEADS])).then_inc(c_ld, 16)
            sp.dma_start(g_mid[:, 0:ATT], a["g_att_out"][0:1, :].broadcast_to([P, ATT])).then_inc(c_ld, 16)
            sp.dma_start(g_mid[:, ATT:D], a["g_pool_out"][0:1, :].broadcast_to([P, POOL])).then_inc(c_ld, 16)
            sp.dma_start(resid[:, 1:2, :], a["x_prompt"][0, P:2 * P, :].rearrange("(t p) d -> p t d", p=P)).then_inc(
                x1_ld, 16)
            sp.dma_start(w_out[:], a["w_out"][0].rearrange("(p k) n -> p k n", k=KC)).then_inc(wout_ld, 16)
            sp.dma_start(resid[:, 2:PROMPT_TILES, :],
                         a["x_prompt"][0, 2 * P:SEQ, :].rearrange("(t p) d -> p t d", p=P)).then_inc(x_ld, 16)
            sp.dma_start(resid[0:NS, SAMPLE, :], a["x_sample"].rearrange("b s d -> (b s) d")).then_inc(x_ld, 16)
            sp.dma_start(smask[:], c["smask"]).then_inc(late_ld, 16)
            sp.dma_start(pmat_s, c["pmat_s"]).then_inc(late_ld, 16)
            sp.dma_start(ustate, a["state_pool"][0].rearrange("b r u -> (b r) u")).then_inc(late_ld, 16)
            sp.dma_start(pick[:], c["pick"]).then_inc(late_ld, 16)
            sp.dma_start(vc, a["cache_v"][0].rearrange("b p g d -> p b (g d)")).then_inc(cache_ld, 16)
            for src, dst in ((a["cache_k"], o["k_sample"]), (a["cache_v"], o["v_sample"])):
                sp.dma_start(dst[0, :, 0:WINDOW - STEPS], src[0, :, STEPS:WINDOW]).then_inc(copied, 16)
            sp.dma_start(o["pool_sample"][0, :, 0:PREFIX - STEPS],
                         a["state_pool"][0, :, STEPS:PREFIX]).then_inc(copied, 16)
            sp.dma_start(keep["raw_g"][:], a["w_exp_gate"][0, 0].rearrange("(p k) f -> p k f", k=KC)).then_inc(
                keep["g_ld"], 16)
            sp.dma_start(keep["raw_u"][:], a["w_exp_up"][0, 0].rearrange("(p k) f -> p k f", k=KC)).then_inc(
                keep["u_ld"], 16)
            sp.wait_ge(roped, PROMPT_TILES)
            sp.wait_ge(zk_ev, 2 * PROMPT_TILES)
            sp.dma_start(o["k_prompt"][0, 0].rearrange("w g d -> w (g d)"), z[:, K0:V0]).then_inc(kv_out, 16)
            sp.dma_start(o["v_prompt"][0, 0].rearrange("w g d -> w (g d)"), z[:, V0:U0]).then_inc(kv_out, 16)
            sp.dma_start(o["pool_prompt"][0, 0], z[P - PREFIX:P, U0:IN_W]).then_inc(kv_out, 16)
            sp.wait_ge(o_done, PROMPT_TILES)
            sp.dma_start(kc, a["cache_k"][0].rearrange("b p g d -> p b (g d)")).then_inc(cache_ld, 16)
            sp.wait_ge(z_done, 3 * TILES)
            for dst, src in router_weights(a, c, keep).values():
                sp.dma_start(dst, src).then_inc(keep["router_ld"], 16)
            sp.wait_ge(roped, TILES)
            sp.wait_ge(zk_ev, 2 * TILES)
            for b in range(SEQS):
                r = slice(b * STEPS, (b + 1) * STEPS)
                new = slice(WINDOW - STEPS, WINDOW)
                sp.dma_start(o["k_sample"][0, b, new].rearrange("w g d -> w (g d)"), z[r, K0:V0]).then_inc(copied, 16)
                sp.dma_start(o["v_sample"][0, b, new].rearrange("w g d -> w (g d)"), z[r, V0:U0]).then_inc(copied, 16)
                sp.dma_start(o["pool_sample"][0, b, PREFIX - STEPS:PREFIX], z[r, U0:IN_W]).then_inc(copied, 16)
            sp.wait_ge(os_ready, 1)
            sp.dma_start(o_dram.rearrange("c p d -> p c d"), o_s).then_inc(o_st, 16)
            sp.wait_ge(o_st, 16)
            sp.wait_ge(o_done, TILES)
            rows_back(sp, range(0, SEQS // 2))
            sp.wait_ge(o_back, 16 * KV_HEADS * SEQS)
            sp.wait_ge(kv_out, 48)
            sp.wait_ge(copied, 16 * (3 + 3 * SEQS))

        @block.gpsimd
        def _(pool):
            pool.memset(resid[NS:P, SAMPLE, :], 0.0).then_inc(zeroed, 1)
            pool.wait_ge(zeroed, 1)
            pool.memset(ident[:], 0.0).then_inc(ident_set, 1)
            pool.wait_ge(ident_set, 1)
            pool.affine_select(out=ident[:], in_=ident[:], compare_op=ALU.not_equal, fill=1.0, base=0,
                               pattern=[[-1, P]], channel_multiplier=1).then_inc(ident_set, 1)
            pool.memset(kT[:, 0:P], 0.0).then_inc(zeroed, 1)
            pool.memset(v_prev[:], 0.0).then_inc(zeroed, 1)
            pool.memset(u_prev[:], 0.0).then_inc(zeroed, 1)

            pool.memset(half[:], -0.5).then_inc(zeroed, 1)
            pool.wait_ge(zeroed, 5)
            own = Chain(pool, pool_own)

            def norm_x(t, n):
                pool_after(pool, keep["passed"], sumsq, t + 1)
                rstd(own, pool, st[0:n, 1:2], st[0:n, 0:1], D, half[0:n, 0:1], x_rstd)

            def norm_mix(t, n):
                pool_after(pool, keep["passed"], mix_sq, 2 * t + 2)
                rstd(own, pool, st[0:n, 4:6], st[0:n, 2:4], ATT, half[0:n, :], m_rstd)

            def keep_previous(t):
                pool_after(pool, keep["passed"], o_done, t + 1)
                pool.tensor_copy(kT[:, 0:P], kT[:, P:2 * P]).then_inc(prev_copied, 1)
                pool.tensor_copy(v_prev[:], z[:, V0:U0]).then_inc(prev_copied, 1)
                pool.tensor_copy(u_prev[:], z[:, U0:IN_W]).then_inc(prev_copied, 1)

            norm_x(0, P)
            own.clear()
            with pool.Fori(0, LAST_PROMPT) as t:
                norm_x(t + 1, P)
                norm_mix(t, P)
                keep_previous(t)
                own.clear()
            norm_x(SAMPLE, NS)
            norm_mix(LAST_PROMPT, P)
            keep_previous(LAST_PROMPT)
            norm_mix(SAMPLE, NS)

        @block.tensor
        def _(pe):
            def transposes(n, done):
                for b in range(2):
                    for k in range(4):
                        ins = pe.transpose(X[b][:, k * n:(k + 1) * n], row[0:n, (4 * b + k) * P:(4 * b + k + 1) * P],
                                           ident[0:n, 0:n])
                    ins.then_inc(done, 1)

            def x_transposes(t, n):
                pe.wait_ge(xs_ready, t + 1)
                after(pe, mix_raw, 2 * t - 1)
                transposes(n, x_tr)

            def mix_transposes(t, n):
                pe.wait_ge(mixed, t + 1)
                transposes(n, m_tr)

            def project_in(t, n, i, weights_too=False):
                bank, n0, n1 = Z_IN[i]
                if i == 0:
                    pe.wait_ge(x_ev, 2 * t + 2)
                if weights_too:
                    pe.wait_ge(win_ld[i], 16)
                for k in range(KC):
                    ins = pe.matmul(bank[0:n, 0:n1 - n0], colT[:, k, 0:n], w_in[:, k, n0:n1],
                                    start=(k == 0), stop=(k == KC - 1))
                ins.then_inc(z_done, 1)

            def pool_means(t, n, prev, prev_mat, cur_mat):
                pe.wait_ge(zk_ev, 2 * t + 2)
                after(pe, prev_copied, 3 * t)
                after(pe, added[0], t)
                for g in range(PG):
                    out = Z[0][:, g * n:(g + 1) * n]
                    pe.matmul(out, prev[:, g * P:(g + 1) * P], prev_mat(g), start=True, stop=False)
                    ins = pe.matmul(out, z[0:n, U0 + g * P:U0 + (g + 1) * P], cur_mat(g), start=False, stop=True)
                ins.then_inc(d_done, 1)

            def qk_transposes(t, n):
                pe.wait_ge(roped, t + 1)
                after(pe, m_ev, 2 * t)
                for j in range(GROUP):
                    pe.transpose(X[0][:, j * n:(j + 1) * n], z[0:n, j * P:(j + 1) * P], ident[0:n, 0:n])
                pe.transpose(X[1][:, 0:n], z[0:n, K0:V0], ident[0:n, 0:n]).then_inc(qk_tr, 1)

            def pool_map(t, n):
                pe.wait_ge(dT_ev, t + 1)
                for g in range(PG):
                    ins = pe.matmul(X[0][0:n, g * P:(g + 1) * P], dT[:, g, 0:n] if n == P else
                                    dT[:].rearrange("p g q -> p (g q)")[:, g * n:(g + 1) * n],
                                    w_pool[:, g, :], start=True, stop=True)
                ins.then_inc(y_done, 1)

            def project_out(t, n, half):
                pe.wait_ge(m_ev, 2 * t + 2)
                if isinstance(t, int):
                    after(pe, added[half], t)
                for k in range(KC):
                    ins = pe.matmul(Z[half][0:n, :], colM[:, k, 0:n], w_out[:, k, half * 512:(half + 1) * 512],
                                    start=(k == 0), stop=(k == KC - 1))
                ins.then_inc(proj_done[half], 1)

            def prompt_tile(t, cur, n_next):
                qk_transposes(t, P)
                if isinstance(t, int) and t == 0:
                    pe.wait_ge(c_ld, 16 * NCONST)
                    pe.wait_ge(zeroed, 4)
                pool_means(t, P, u_prev, lambda g: pmat[:, 2, g, :], lambda g: pmat[:, cur, g, :])
                pe.wait_ge(qk_ev, 2 * t + 2)
                after(pe, pt_act, 2 * t)
                after(pe, pt_dve, 2 * t)
                for h in range(HEADS):
                    g, j = divmod(h, GROUP)
                    ins = pe.matmul(S[h // 2][:, (h % 2) * 256:(h % 2) * 256 + 256],
                                    qT[HD * g:HD * g + HD, j, :], kT[HD * g:HD * g + HD, :], start=True, stop=True)
                    if h % 2:
                        ins.then_inc(s_done, 1)
                pool_map(t, P)
                if not (isinstance(t, int) and t == 0):
                    project_out(t - 1, P, 1)
                for h in range(HEADS):
                    if h % 2 == 0:
                        pe.wait_ge(p_ready, 4 * t + h // 2 + 1)
                    for b in range(2):
                        ins = pe.transpose(S[h // 2][:, (h % 2) * 256 + b * P:(h % 2) * 256 + (b + 1) * P],
                                           prob[:, h, b * P:(b + 1) * P], ident[:])
                    if h % 2:
                        ins.then_inc(pt_tr, 1)
                x_transposes(t + 1, n_next)
                pe.wait_ge(pt_dve, 2 * t + 2)
                pe.wait_ge(pt_act, 2 * t + 2)
                for h in range(HEADS):
                    g = h // GROUP
                    out = Z[0][:, h * HD:(h + 1) * HD]
                    pe.matmul(out, probT[:, h, 0, :], v_prev[:, g * HD:(g + 1) * HD], start=True, stop=False)
                    ins = pe.matmul(out, probT[:, h, 1, :], z[:, V0 + g * HD:V0 + (g + 1) * HD],
                                    start=False, stop=True)
                ins.then_inc(o_done, 1)
                project_in(t + 1, n_next, 0)
                project_in(t + 1, n_next, 1)
                mix_transposes(t, P)
                project_in(t + 1, n_next, 2)
                if isinstance(t, int) and t == 0:
                    pe.wait_ge(wout_ld, 16)
                project_out(t, P, 0)

            def sample_tile(t):
                n = NS
                nst = SEQS * PREFIX
                pe.wait_ge(late_ld, 16 * 4)
                pe.wait_ge(zk_ev, 2 * t + 2)
                pe.wait_ge(cache_ld, 32)
                for b in range(SEQS):
                    ins = pe.transpose(S[2 + b // 4][:, (b % 4) * P:(b % 4 + 1) * P], kc[:, b, :], ident[:])
                ins.then_inc(kc_tr, 1)
                qk_transposes(t, n)
                pool_means(t, n, ustate, lambda g: pmat_s[0:nst, 1, g, :], lambda g: pmat_s[0:n, 0, g, :])
                pe.wait_ge(qk_ev, 2 * t + 2)
                pe.wait_ge(kc_ev, 2)
                for ch in range(4):
                    half, g = divmod(ch, KV_HEADS)
                    for i in range(4):
                        b = 4 * half + i
                        q = qT[:].rearrange("p j q -> p (j q)")[HD * g:HD * g + HD, 32 * b:32 * b + 32]
                        rows = slice(32 * i, 32 * i + 32)
                        pe.matmul(S[ch][rows, 0:P], q, kcT[HD * g:HD * g + HD, b, :], start=True, stop=True)
                        ins = pe.matmul(S[ch][rows, P:P + n], q, kT[HD * g:HD * g + HD, P:P + n],
                                        start=True, stop=True)
                    ins.then_inc(s_done, 1)
                pool_map(t, n)
                project_out(t - 1, P, 1)
                pe.wait_ge(p_ready, 4 * t + 4)
                for ch in range(4):
                    pe.transpose(S[ch][:, 0:P], prob_s[:, ch, 0:P], ident[:])
                    ins = pe.transpose(S[ch][0:n, P:2 * P], prob_s[:, ch, P:P + n], ident[:])
                    ins.then_inc(pt_tr, 1)
                pe.wait_ge(pts_ev, 9)
                for ch in range(4):
                    half, g = divmod(ch, KV_HEADS)
                    for i in range(4):
                        out = Z[0][32 * i:32 * i + 32, ch * HD:(ch + 1) * HD]
                        pe.matmul(out, ptc[:, ch, 32 * i:32 * i + 32], vc[:, 4 * half + i, g * HD:(g + 1) * HD],
                                  start=True, stop=False)
                        ins = pe.matmul(out, ptn[0:n, ch, 32 * i:32 * i + 32], z[0:n, V0 + g * HD:V0 + (g + 1) * HD],
                                        start=False, stop=True)
                ins.then_inc(o_done, 1)
                mix_transposes(t, n)
                project_out(t, n, 0)
                project_out(t, n, 1)

            pe.wait_ge(ident_set, 2)
            x_transposes(0, P)
            for i in range(3):
                project_in(0, P, i, weights_too=True)
            prompt_tile(0, 0, P)
            with pe.Fori(1, LAST_PROMPT) as t:
                prompt_tile(t, 1, P)
            prompt_tile(LAST_PROMPT, 1, NS)
            sample_tile(SAMPLE)

        @block.scalar
        def _(act):
            def square_sum(t, n, src):
                after(act, xs_ready, t)
                after(act, mix_sq, 2 * t - 2)
                act.activation(junk[0:n, :], src, ACT.Square, accum_out=st[0:n, 0:1]).then_inc(sumsq, 1)

            def col_copy(dst, t, n, tr, ev):
                act.wait_ge(tr, 2 * t + 1)
                act.activation(dst[:, 0:4, 0:n], X[0][:, 0:4 * n].rearrange("p (k q) -> p k q", k=4),
                               ACT.Copy).then_inc(ev, 1)

            def z_copy(t, n, i):
                bank, n0, n1 = Z_IN[i]
                if i == 1:
                    after(act, prev_copied, 3 * t)
                act.wait_ge(z_done, 3 * t + i + 1)
                act.activation(z[0:n, n0:n1], bank[0:n, 0:n1 - n0], ACT.Copy).then_inc(zk_ev, 1)

            def dT_copy(t, n):
                act.wait_ge(d_done, t + 1)
                act.activation(dT[:].rearrange("p g q -> p (g q)")[:, 0:PG * n], Z[0][:, 0:PG * n],
                               ACT.Copy).then_inc(dT_ev, 1)

            def k_copy(t, n):
                act.wait_ge(qk_tr, t + 1)
                act.activation(kT[:, P:P + n], X[1][:, 0:n], ACT.Copy).then_inc(qk_ev, 1)

            def mix_squares(t, n):
                act.wait_ge(mix_raw, 2 * t + (2 if n == P else 1))
                act.wait_ge(sumsq, t + 2 if n == P else TILES)
                after(act, mixed, t)
                act.activation(junk[0:n, 0:ATT], mix[0:n, 0:ATT], ACT.Square, accum_out=st[0:n, 2:3]).then_inc(mix_sq, 1)
                act.activation(junk[0:n, ATT:D], mix[0:n, ATT:D], ACT.Square, accum_out=st[0:n, 3:4]).then_inc(mix_sq, 1)

            def prompt_tile(t, next_src, n_next):
                k_copy(t, P)
                dT_copy(t, P)
                square_sum(t + 1, n_next, next_src)
                act.wait_ge(m_ready, t + 1)
                for h in range(HEADS):
                    ins = act.activation(prob[:, h, :], prob[:, h, :], ACT.Exp, bias=m8[:, 1, h:h + 1],
                                         accum_out=den[:, h:h + 1])
                    if h == HEADS - 1:
                        act.activation(m8[:, 2, :], m8[:, 2, :], ACT.Exp).then_inc(p_ready, 1)
                    elif h % 2:
                        ins.then_inc(p_ready, 1)
                for b in (2, 3):
                    act.wait_ge(pt_tr, 4 * t + b + 1)
                    act.activation(probT[:, 2 * b:2 * b + 2].rearrange("p h b q -> p (h b q)"), S[b][:],
                                   ACT.Copy).then_inc(pt_act, 1)
                col_copy(colT, t + 1, n_next, x_tr, x_ev)
                mix_squares(t, P)
                if n_next == NS:
                    act.wait_ge(kv_out, 48)
                z_copy(t + 1, n_next, 1)
                col_copy(colM, t, P, m_tr, m_ev)
                z_copy(t + 1, n_next, 2)

            def sample_tile(t):
                n = NS
                act.wait_ge(kc_tr, 1)
                for i in range(2):
                    act.activation(kcT[:, 4 * i:4 * i + 4, :].rearrange("p b k -> p (b k)"), S[2 + i][:],
                                   ACT.Copy).then_inc(kc_ev, 1)
                k_copy(t, n)
                dT_copy(t, n)
                act.wait_ge(m_ready, t + 1)
                for ch in range(4):
                    act.activation(prob_s[:, ch, :], prob_s[:, ch, :], ACT.Exp, bias=m8[:, 1, ch:ch + 1],
                                   accum_out=den[:, ch:ch + 1]).then_inc(p_ready, 1)
                act.activation(m8[:, 2, 0:4], m8[:, 2, 0:4], ACT.Exp).then_inc(pts_ev, 1)
                for ch in range(4):
                    act.wait_ge(pt_tr, 4 * t + ch + 1)
                    act.activation(ptc[:, ch, :], S[ch][:, 0:P], ACT.Copy).then_inc(pts_ev, 1)
                    act.activation(ptn[0:n, ch, :], S[ch][0:n, P:2 * P], ACT.Copy).then_inc(pts_ev, 1)
                act.wait_ge(o_st, 16)
                act.wait_ge(o_done, TILES)
                rows_back(act, range(SEQS // 2, SEQS))
                act.wait_ge(o_back, 16 * KV_HEADS * SEQS)
                mix_squares(t, n)
                col_copy(colM, t, n, m_tr, m_ev)

            act.wait_ge(x0_ld, 16)
            square_sum(0, P, resid[:, 0, :])
            col_copy(colT, 0, P, x_tr, x_ev)
            z_copy(0, P, 1)
            z_copy(0, P, 2)
            act.wait_ge(x1_ld, 16)
            prompt_tile(0, resid[:, 1, :], P)
            act.wait_ge(x_ld, 32)
            with act.Fori(1, LAST_PROMPT) as t:
                prompt_tile(t, resid[:, t + 1, :], P)
            prompt_tile(LAST_PROMPT, resid[0:NS, SAMPLE, :], NS)
            sample_tile(SAMPLE)

        @block.vector
        def _(dve):
            own = Chain(dve, dve_own)

            def norm_in(t, n, src):
                dve.wait_ge(x_rstd, t + 1)
                after(dve, m_tr, 2 * t - 2)
                dve.scalar_tensor_tensor(out=row[0:n, :].rearrange("p (k q) -> p q k", k=KC),
                                         in0=src.rearrange("p (q k) -> p q k", k=KC), scalar=st[0:n, 1:2],
                                         in1=g_mix[0:n, :].rearrange("p (q k) -> p q k", k=KC),
                                         op0=ALU.mult, op1=ALU.mult).then_inc(xs_ready, 1)

            def col_copy(dst, t, n, tr, ev):
                dve.wait_ge(tr, 2 * t + 2)
                dve.tensor_copy(dst[:, 4:8, 0:n],
                                X[1][:, 0:4 * n].rearrange("p (k q) -> p k q", k=4)).then_inc(ev, 1)

            def rotate(t, n):
                dve.wait_ge(z_done, 3 * t + 1)
                own.did(dve.tensor_copy(z[0:n, 0:ATT].rearrange("p (j g d) -> p g j d", j=GROUP, d=HD),
                                        Z_IN[0][0][0:n, :].rearrange("p (g j d) -> p g j d", j=GROUP, d=HD)))
                own.wait()
                dve.wait_ge(zk_ev, 2 * t + 1)
                heads = HEADS + KV_HEADS
                hv = z[0:n, 0:V0].rearrange("p (h d) -> p h d", d=HD)
                x1, x2 = hv[:, :, 0:HALF], hv[:, :, HALF:2 * HALF]
                cs = [rope[0:n, t, i:i + 1, :].broadcast_to([n, heads, HALF]) for i in range(2)]
                for i, (x, f) in enumerate(((x1, 0), (x2, 1), (x2, 0), (x1, 1))):
                    own.did(dve.tensor_tensor(rt[0:n, i], x, cs[f], ALU.mult))
                own.wait()
                own.did(dve.tensor_tensor(x1, rt[0:n, 0], rt[0:n, 1], ALU.subtract))
                dve.tensor_tensor(x2, rt[0:n, 2], rt[0:n, 3], ALU.add).then_inc(roped, 1)

            def q_copy(t, n):
                dve.wait_ge(qk_tr, t + 1)
                dst, src = qT[:].rearrange("p j q -> p (j q)")[:, 0:GROUP * n], X[0][:, 0:GROUP * n]
                if n != P:
                    dst = dst.rearrange("p (b j s) -> p j b s", j=GROUP, s=STEPS)
                    src = src.rearrange("p (j b s) -> p j b s", j=GROUP, s=STEPS)
                dve.tensor_copy(dst, src).then_inc(qk_ev, 1)

            def softmax_head(t, n_sets, sinks):
                own.wait()
                own.did(dve.tensor_tensor(m8[:, 0, 0:n_sets], mx[:, 0:n_sets], sinks, ALU.max))
                own.wait()
                own.did(dve.tensor_tensor(m8[:, 2, 0:n_sets], sinks, m8[:, 0, 0:n_sets], ALU.subtract))
                own.wait()
                dve.tensor_scalar(m8[:, 1, 0:n_sets], m8[:, 0, 0:n_sets], -1.0, None, ALU.mult).then_inc(m_ready, 1)

            def denominators(n_sets):
                own.did(dve.tensor_tensor(den[:, 0:n_sets], den[:, 0:n_sets], m8[:, 2, 0:n_sets], ALU.add))
                own.wait()
                own.did(dve.reciprocal(rden[:, 0:n_sets], den[:, 0:n_sets]))
                own.wait()

            def pool_scale(t, n):
                dve.wait_ge(y_done, t + 1)
                dve.tensor_tensor(mix[0:n, ATT:D], X[0][0:n, :], p_scale[0:n, :], ALU.mult).then_inc(mix_raw, 1)

            def mix_norm(t, n):
                dve.wait_ge(m_rstd, t + 1)
                for i in range(2):
                    w = slice(i * ATT, (i + 1) * ATT)
                    ins = dve.scalar_tensor_tensor(
                        out=row[0:n, :].rearrange("p (k q) -> p q k", k=KC)[:, i * 64:(i + 1) * 64, :],
                        in0=mix[0:n, w].rearrange("p (q k) -> p q k", k=KC), scalar=st[0:n, 4 + i:5 + i],
                        in1=g_mid[0:n, w].rearrange("p (q k) -> p q k", k=KC), op0=ALU.mult, op1=ALU.mult)
                    if i == 0:
                        own.did(ins)
                own.wait()
                ins.then_inc(mixed, 1)

            def add_residual(n, dst, done, half):
                dve.wait_ge(proj_done[half], done)
                w = slice(half * 512, (half + 1) * 512)
                dve.tensor_tensor(dst[:, w], Z[half][0:n, :], dst[:, w], ALU.add).then_inc(added[half], 1)

            def prompt_tile(t, mask, next_src, n_next):
                q_copy(t, P)
                for b in range(4):
                    dve.wait_ge(s_done, 4 * t + b + 1)
                    own.did(dve.scalar_tensor_tensor(
                        out=prob[:, 2 * b:2 * b + 2, :], in0=S[b][:].rearrange("p (h k) -> p h k", h=2), scalar=SCALE,
                        in1=amask[:, mask:mask + 1, :].broadcast_to([P, 2, 2 * P]), op0=ALU.mult, op1=ALU.add))
                    own.wait()
                    own.did(dve.tensor_reduce(mx[:, 2 * b:2 * b + 2], prob[:, 2 * b:2 * b + 2, :], AX.X, ALU.max))
                softmax_head(t, HEADS, sink[:])
                norm_in(t + 1, n_next, next_src)
                pool_scale(t, P)
                if not (isinstance(t, int) and t == 0):
                    add_residual(P, resid[:, t - 1, :], t, 1)
                for b in (0, 1):
                    dve.wait_ge(pt_tr, 4 * t + b + 1)
                    dve.tensor_copy(probT[:, 2 * b:2 * b + 2].rearrange("p h b q -> p (h b q)"),
                                    S[b][:]).then_inc(pt_dve, 1)
                dve.wait_ge(p_ready, 4 * t + 4)
                denominators(HEADS)
                col_copy(colT, t + 1, n_next, x_tr, x_ev)
                dve.wait_ge(o_done, t + 1)
                dve.tensor_tensor(mix[:, 0:ATT].rearrange("p (h d) -> p h d", d=HD),
                                  Z[0][:].rearrange("p (h d) -> p h d", d=HD),
                                  rden[:, :].rearrange("p (h q) -> p h q", q=1).broadcast_to([P, HEADS, HD]),
                                  ALU.mult).then_inc(mix_raw, 1)
                mix_norm(t, P)
                col_copy(colM, t, P, m_tr, m_ev)
                if n_next == NS:
                    dve.wait_ge(kv_out, 48)
                rotate(t + 1, n_next)
                add_residual(P, resid[:, t, :], t + 1, 0)
                own.clear()

            def sample_tile(t):
                n = NS
                q_copy(t, n)
                for ch in range(4):
                    dve.wait_ge(s_done, 4 * t + ch + 1)
                    own.did(dve.scalar_tensor_tensor(out=prob_s[:, ch, :], in0=S[ch][:, 0:P + n], scalar=SCALE,
                                                     in1=smask[:, ch // 2, :], op0=ALU.mult, op1=ALU.add))
                    own.wait()
                    own.did(dve.tensor_reduce(mx[:, ch:ch + 1], prob_s[:, ch, :], AX.X, ALU.max))
                own.did(dve.tensor_tensor(picked[:], pick[:], sink[:, :].rearrange("p (a h) -> p a h", a=1).broadcast_to(
                    [P, KV_HEADS, HEADS]), ALU.mult))
                own.wait()
                own.did(dve.tensor_reduce(sink_s[:], picked[:], AX.X, ALU.add))
                own.wait()
                for half in range(2):
                    own.did(dve.tensor_copy(m8[:, 1, 2 * half:2 * half + 2], sink_s[:]))
                own.wait()
                own.did(dve.tensor_tensor(m8[:, 0, 0:4], mx[:, 0:4], m8[:, 1, 0:4], ALU.max))
                own.wait()
                own.did(dve.tensor_tensor(m8[:, 2, 0:4], m8[:, 1, 0:4], m8[:, 0, 0:4], ALU.subtract))
                own.wait()
                dve.tensor_scalar(m8[:, 1, 0:4], m8[:, 0, 0:4], -1.0, None, ALU.mult).then_inc(m_ready, 1)
                pool_scale(t, n)
                add_residual(P, resid[:, t - 1, :], t, 1)
                dve.wait_ge(pts_ev, 9)
                denominators(4)
                dve.wait_ge(o_done, t + 1)
                dve.tensor_tensor(o_s, Z[0][:, 0:4 * HD].rearrange("p (c d) -> p c d", c=4),
                                  rden[:, 0:4].rearrange("p (c q) -> p c q", q=1).broadcast_to([P, 4, HD]),
                                  ALU.mult).then_inc(os_ready, 1)
                dve.wait_ge(o_back, 16 * KV_HEADS * SEQS)
                mix_norm(t, n)
                col_copy(colM, t, n, m_tr, m_ev)
                for half in range(2):
                    add_residual(n, resid[0:n, t, :], t + 1, half)

            dve.wait_ge(x0_ld, 16)
            dve.wait_ge(g_mix_ld, 16)
            norm_in(0, P, resid[:, 0, :])
            col_copy(colT, 0, P, x_tr, x_ev)
            dve.wait_ge(c_ld, 16 * NCONST)
            rotate(0, P)
            own.clear()
            prompt_tile(0, 0, resid[:, 1, :], P)
            dve.wait_ge(x_ld, 32)
            with dve.Fori(1, LAST_PROMPT) as t:
                prompt_tile(t, 1, resid[:, t + 1, :], P)
            dve.wait_ge(zeroed, 4)
            dve.wait_ge(late_ld, 16 * 4)
            prompt_tile(LAST_PROMPT, 1, resid[0:NS, SAMPLE, :], NS)
            sample_tile(SAMPLE)




def router(nc, a, c, keep, rows_dram, y_dram):
    resid, ident, place, w8, slots, rounds, y_row = (
        keep[n] for n in ("resid", "ident", "place", "w8", "slots", "rounds", "y_row"))
    LAST = TILES - 1
    with ExitStack() as ctx:
        def sb(name, shape, dt=F32):
            return ctx.enter_context(nc.sbuf_tensor(name, shape, dt))

        def sem(name):
            return ctx.enter_context(nc.semaphore(name))

        w_r, s_gate, s_up, s_down, g_ffn, bias, tri_f, iota_e, valid = (
            router_weights(a, c, keep)[n][0] for n in (
                "w_r", "s_gate", "s_up", "s_down", "g_ffn", "bias", "tri_f", "iota_e", "valid"))
        tri = sb("tri", [P, P], BF16)
        ones = sb("ones", [P, P], BF16)
        row = sb("row2", [P, D])
        colT = sb("colT2", [P, KC, P])
        junk = sb("junk2", [P, D], BF16)
        st = sb("st2", [P, 4])
        half = sb("half2", [P, 1])
        iota1_f = sb("iota1_f", [P, CAP])
        tok_f = sb("tok_f", [P, TILES, 2])
        zero = sb("zero", [P, D])
        sg = sb("sg", [P, 2, 2 * P])
        hid = sb("hid", [P, FC, P])
        score = sb("score", [P, E])
        biased = sb("biased", [P, E])
        top2 = sb("top2", [P, EG, 8])
        grp = sb("grp", [P, EG])
        gv = sb("gv", [P, 8])
        gi = sb("gi", [P, 8], U32)
        gif = sb("gif", [P, 8])
        geq = sb("geq", [P, EG, TOP_GROUPS])
        pen = sb("pen", [P, EG])
        v8 = sb("v8", [P, 8])
        i8 = sb("i8", [P, 8], U32)
        idx8 = sb("idx8", [P, TILES, TOP])
        pos8 = sb("pos8", [P, TILES, TOP])
        hot = sb("hot", [P, TOP, E])
        prod = sb("prod", [P, TOP, E])
        maskf = sb("maskf", [P, E])
        maskb = sb("maskb", [P, E], BF16)
        sofar = sb("sofar", [P, E], BF16)
        pe_pos = sb("pe_pos", [P, E])
        sel8 = sb("sel8", [P, TOP])
        sums = sb("sums", [P, 2])
        tmp = sb("tmp", [P, 2, TILES * TOP])
        top = sb("top", [1, 2])
        limits = sb("limits", [1, 2, ROUNDS - 1])
        cnt = sb("cnt", [1, 6, E])
        one_f = sb("one_f", [1, P])
        shift = sb("shift", [P, E])

        X = [ctx.enter_context(nc.psum_tensor(f"RX{i}", [P, 512], F32)) for i in range(2)]
        R, G, U, C = (ctx.enter_context(nc.psum_tensor(n, [P, 512], F32)) for n in ("RR", "RG", "RU", "RC"))
        Y = [ctx.enter_context(nc.psum_tensor(f"RY{i}", [P, 512], F32)) for i in range(2)]

        sumsq, row_ready, row_st, x_tr, x_ev, r_done, g_done, u_done, e_ready, s_ready, h_ready, y_done = (
            sem(n) for n in ("sumsq2", "row_ready", "row_st", "x_tr2", "x_ev2", "r_done", "g_done", "u_done",
                             "e_ready", "s_ready", "h_ready2", "y_done2"))
        y_added, mask_ready, placed, consts, count_done = (
            sem(n) for n in ("y_added", "mask_ready", "placed", "consts2", "count_done"))
        shift_ready, rounds_known, cleared = sem("shift_ready"), sem("rounds_known"), sem("cleared")
        list_ld = sem("list_ld")
        dve_own, pool_own, rstd_ready = sem("dve_own_router"), sem("pool_own_router"), sem("rstd_ready2")

        block = ctx.enter_context(nc.Block())

        @block.sync
        def _(sp):
            sp.dma_start(keep["raw_d"][:], a["w_exp_down"][0, 0].rearrange("(f p) d -> p f d", p=P)).then_inc(
                keep["d_ld"], 16)
            sp.dma_start(iota1_f[:], c["iota1"]).then_inc(list_ld, 16)
            sp.dma_start(tok_f[:], c["tok"]).then_inc(list_ld, 16)
            with sp.Fori(0, TILES) as t:
                at = sp.snap(t * P)
                sp.wait_ge(row_ready, t + 1)
                sp.dma_start(rows_dram[bass.ds(at, P)], row[:]).then_inc(row_st, 16)
            sp.wait_ge(row_st, 16 * TILES)
            sp.wait_ge(rounds_known, 1)
            n_rounds = sp.value_load(rounds[0:1, 0:1], min_val=1, max_val=ROUNDS)
            with sp.If(n_rounds > 1):
                whole = (Y_ROWS - OVER_ROW) // P
                with sp.Fori(0, whole) as i:
                    at = sp.snap(i * P + OVER_ROW)
                    sp.dma_start(y_dram[bass.ds(at, P)], zero[:]).then_inc(cleared, 16)
                rest = Y_ROWS - OVER_ROW - whole * P
                sp.dma_start(y_dram[Y_ROWS - rest:Y_ROWS], zero[0:rest, :]).then_inc(cleared, 16)
                sp.wait_ge(cleared, 16 * whole + 16)

        @block.gpsimd
        def _(pool):
            own = Chain(pool, pool_own)

            def norm(t):
                pool_after(pool, keep["passed"], sumsq, t + 1)
                rstd(own, pool, st[:, 2:3], st[:, 0:1], D, half[:], rstd_ready)
                own.clear()

            pool.memset(half[:], -0.5).then_inc(consts, 1)
            pool.wait_ge(consts, 1)
            norm(0)
            pool.memset(ones[:], 1.0).then_inc(consts, 1)
            pool.memset(sofar[:], 0.0).then_inc(consts, 1)
            pool.memset(place[:, E:E + 3, :], 0.0).then_inc(consts, 1)
            pool.memset(zero[:], 0.0).then_inc(consts, 1)
            pool.wait_ge(consts, 5)
            with pool.Fori(1, TILES) as t:
                norm(t)
            pool.wait_ge(list_ld, 32)
            own.did(pool.tensor_copy(keep["iota1"][:], iota1_f[:]))
            own.did(pool.tensor_copy(keep["tok"][:], tok_f[:]))
            own.wait()

        @block.tensor
        def _(pe):
            def transposes(t):
                pe.wait_ge(row_ready, t + 1)
                after(pe, x_ev, 2 * t)
                for b in range(2):
                    for k in range(4):
                        ins = pe.transpose(X[b][:, k * P:(k + 1) * P], row[:, (4 * b + k) * P:(4 * b + k + 1) * P],
                                           ident[:])
                    ins.then_inc(x_tr, 1)

            def tile(t, following):
                pe.wait_ge(x_ev, 2 * t + 2)
                after(pe, s_ready, t)
                for k in range(KC):
                    ins = pe.matmul(R[:, 0:E], colT[:, k, :], w_r[:, k, :], start=(k == 0), stop=(k == KC - 1))
                ins.then_inc(r_done, 1)
                after(pe, h_ready, t)
                for bank, w, done in ((G, s_gate, g_done), (U, s_up, u_done)):
                    for f in range(FC):
                        for k in range(KC):
                            ins = pe.matmul(bank[:, f * P:(f + 1) * P], w[:, k, f * P:(f + 1) * P], colT[:, k, :],
                                            start=(k == 0), stop=(k == KC - 1))
                    ins.then_inc(done, 1)
                following()
                pe.wait_ge(mask_ready, t + 1)
                after(pe, placed, t)
                pe.matmul(C[:, 0:E], tri[:], maskb[:], start=True, stop=False)
                pe.matmul(C[:, 0:E], ones[:], sofar[:], start=False, stop=True).then_inc(count_done, 1)
                pe.wait_ge(h_ready, t + 1)
                after(pe, y_added, 2 * t)
                for half in range(2):
                    for f in range(FC):
                        ins = pe.matmul(Y[half][:], hid[:, f, :], s_down[:, f, half * 512:(half + 1) * 512],
                                        start=(f == 0), stop=(f == FC - 1))
                    ins.then_inc(y_done, 1)

            transposes(0)
            pe.wait_ge(keep["router_ld"], 16 * 9)
            pe.wait_ge(consts, 5)
            tile(0, lambda: transposes(1))
            with pe.Fori(1, LAST) as t:
                tile(t, lambda: transposes(t + 1))
            tile(LAST, lambda: None)
            pe.wait_ge(placed, TILES)
            pe.matmul(C[0:1, 0:E], ones[:, 0:1], sofar[:], start=True, stop=True).then_inc(count_done, 1)
            pe.wait_ge(rounds_known, 1)
            n_rounds = pe.value_load(rounds[0:1, 0:1], min_val=1, max_val=ROUNDS)
            with pe.If(n_rounds > 1):
                pe.wait_ge(shift_ready, 1)
                pe.matmul(C[:, 0:E], one_f[:], cnt[:, 5, :], start=True, stop=True).then_inc(count_done, 1)

        @block.scalar
        def _(act):
            def square_sum(t):
                after(act, row_ready, t)
                act.activation(junk[:], resid[:, t, :], ACT.Square, accum_out=st[:, 0:1]).then_inc(sumsq, 1)

            def col_copy(t):
                for b in range(2):
                    act.wait_ge(x_tr, 2 * t + b + 1)
                    act.activation(colT[:, 4 * b:4 * b + 4, :], X[b][:].rearrange("p (k q) -> p k q", k=4),
                                   ACT.Copy).then_inc(x_ev, 1)

            def tile(t, following):
                act.wait_ge(r_done, t + 1)
                act.activation(score[:], R[:, 0:E], ACT.Exp, scale=-1.0).then_inc(e_ready, 1)
                act.wait_ge(g_done, t + 1)
                act.activation(sg[:, 0, :], G[:, 0:FC * P], ACT.Sigmoid).then_inc(e_ready, 1)
                following()

            def following(t, two):
                act.wait_ge(u_done, t + 1)
                col_copy(t + 1)
                if two:
                    square_sum(t + 2)

            square_sum(0)
            for name in "gud":
                act.wait_ge(keep[f"{name}_ld"], 16)
                for part in range(HI_PARTS[name]):
                    split_hi(act, keep, name, 0, part)
                if name == "u":
                    col_copy(0)
                    square_sum(1)
            tile(0, lambda: following(0, True))
            with act.Fori(1, LAST - 1) as t:
                tile(t, lambda: following(t, True))
            tile(LAST - 1, lambda: following(LAST - 1, False))
            tile(LAST, lambda: None)

        @block.vector
        def _(dve):
            own = Chain(dve, dve_own)

            def norm(t):
                dve.wait_ge(rstd_ready, t + 1)
                after(dve, row_st, 16 * t)
                after(dve, x_tr, 2 * t)
                dve.scalar_tensor_tensor(out=row[:].rearrange("p (k q) -> p q k", k=KC),
                                         in0=resid[:, t, :].rearrange("p (q k) -> p q k", k=KC), scalar=st[:, 2:3],
                                         in1=g_ffn.rearrange("p (q k) -> p q k", k=KC),
                                         op0=ALU.mult, op1=ALU.mult).then_inc(row_ready, 1)

            def hot_sum(factor, dst):
                own.did(dve.tensor_tensor(prod[:], hot[:], factor.rearrange("p (a e) -> p a e", a=1).broadcast_to(
                    [P, TOP, E]), ALU.mult))
                own.wait()
                own.did(dve.tensor_reduce(dst, prod[:], AX.X, ALU.add))
                own.wait()

            def choose(t):
                dve.wait_ge(e_ready, 2 * t + 1)
                own.did(dve.tensor_scalar(score[:], score[:], 1.0, None, ALU.add))
                own.wait()
                own.did(dve.reciprocal(score[:], score[:]))
                own.wait()
                own.did(dve.tensor_tensor(biased[:], score[:], bias, ALU.add))
                own.wait()
                for g in range(EG):
                    own.did(dve.max(top2[:, g, :], biased[:, g * EG:(g + 1) * EG]))
                own.wait()
                own.did(dve.tensor_tensor(grp[:], top2[:, :, 0], top2[:, :, 1], ALU.add))
                own.wait()
                own.did(dve.max(gv[:], grp[:]))
                own.wait()
                own.did(dve.max_index(gi[:], gv[:], grp[:]))
                own.wait()
                own.did(dve.tensor_copy(gif[:], gi[:]))
                own.wait()
                own.did(dve.tensor_tensor(
                    geq[:], iota_e[:, 0:EG].rearrange("p (g k) -> p g k", k=1).broadcast_to([P, EG, TOP_GROUPS]),
                    gif[:, 0:TOP_GROUPS].rearrange("p (a k) -> p a k", a=1).broadcast_to([P, EG, TOP_GROUPS]),
                    ALU.is_equal))
                own.wait()
                own.did(dve.tensor_reduce(pen[:], geq[:], AX.X, ALU.add))
                own.wait()
                own.did(dve.tensor_scalar(pen[:], pen[:], -NEG, NEG, ALU.mult, ALU.add))
                own.wait()
                own.did(dve.tensor_tensor(
                    biased[:].rearrange("p (g e) -> p g e", g=EG), biased[:].rearrange("p (g e) -> p g e", g=EG),
                    pen[:].rearrange("p (g e) -> p g e", e=1).broadcast_to([P, EG, E // EG]), ALU.add))
                own.wait()
                own.did(dve.max(v8[:], biased[:]))
                own.wait()
                own.did(dve.max_index(i8[:], v8[:], biased[:]))
                own.wait()
                own.did(dve.tensor_copy(idx8[:, t, :], i8[:]))
                own.wait()
                own.did(dve.tensor_tensor(
                    hot[:], iota_e.rearrange("p (a e) -> p a e", a=1).broadcast_to([P, TOP, E]),
                    idx8[:, t, :].rearrange("p (k e) -> p k e", e=1).broadcast_to([P, TOP, E]), ALU.is_equal))
                own.wait()
                own.did(dve.tensor_reduce(maskf[:], hot[:].rearrange("p k e -> p e k"), AX.X, ALU.add))
                own.wait()
                own.did(dve.tensor_scalar(maskf[:], maskf[:], valid[:, bass.ds(t, 1)], None, ALU.mult))
                own.wait()
                dve.tensor_copy(maskb[:], maskf[:]).then_inc(mask_ready, 1)

            def weights(t):
                hot_sum(score[:], sel8[:])
                own.did(dve.tensor_reduce(sums[:, 0:1], sel8[:], AX.X, ALU.add))
                own.wait()
                own.did(dve.reciprocal(sums[:, 1:2], sums[:, 0:1]))
                own.wait()
                dve.tensor_scalar(w8[:, t, :], sel8[:], sums[:, 1:2], ROUTED_SCALE, ALU.mult,
                                  ALU.mult).then_inc(s_ready, 1)

            def places(t):
                dve.wait_ge(count_done, t + 1)
                own.did(dve.scalar_tensor_tensor(out=pe_pos[:], in0=C[:, 0:E], scalar=1.0, in1=maskf[:],
                                                 op0=ALU.add, op1=ALU.mult))
                own.wait()
                own.did(dve.tensor_copy(place[:, 0:E, t], pe_pos[:]))
                own.did(dve.tensor_tensor(sofar[:], sofar[:], maskf[:], ALU.add))
                hot_sum(pe_pos[:], pos8[:, t, :])
                own.wait()
                dve.tensor_copy(sums[:, 0:1], sums[:, 1:2]).then_inc(placed, 1)

            def shared(t):
                dve.wait_ge(e_ready, 2 * t + 2)
                own.did(dve.tensor_tensor(sg[:, 1, :], sg[:, 0, :], G[:, 0:FC * P], ALU.mult))
                own.wait()
                dve.wait_ge(u_done, t + 1)
                dve.tensor_tensor(hid[:].rearrange("p f q -> p (f q)"), sg[:, 1, :], U[:, 0:FC * P],
                                  ALU.mult).then_inc(h_ready, 1)

            def tile(t, then):
                choose(t)
                shared(t)
                weights(t)
                places(t)
                for half in range(2):
                    dve.wait_ge(y_done, 2 * t + half + 1)
                    w = slice(half * 512, (half + 1) * 512)
                    dve.tensor_tensor(resid[:, t, w], Y[half][:], resid[:, t, w], ALU.add).then_inc(y_added, 1)
                then()
                own.clear()

            dve.wait_ge(keep["router_ld"], 16 * 9)
            norm(0)
            for name in "gu":
                split_lo(dve, keep, name, 0)
            dve.wait_ge(consts, 5)
            own.did(dve.tensor_copy(tri[:], tri_f))
            own.wait()
            norm(1)
            split_lo(dve, keep, "d", 0)
            tile(0, lambda: norm(2))
            with dve.Fori(1, LAST - 1) as t:
                tile(t, lambda: norm(t + 2))
            tile(LAST - 1, lambda: None)
            tile(LAST, lambda: None)

            row_of = tmp[:, 0, :]
            limit, passed_by = limits[:, 0, :], limits[:, 1, :]
            own.did(dve.scalar_tensor_tensor(out=row_of, in0=idx8[:].rearrange("p t k -> p (t k)"), scalar=float(CAP),
                                             in1=pos8[:].rearrange("p t k -> p (t k)"), op0=ALU.mult, op1=ALU.add))
            own.did(dve.tensor_scalar(limit, iota_e[0:1, 1:ROUNDS], float(CAP), 0.5, ALU.mult, ALU.add))
            own.did(dve.memset(keep["fill"][:, E:ROUNDS * E], CAP))
            own.did(dve.tensor_scalar(y_row[:, 0:E], iota_e[0:1, :], float(CAP), None, ALU.mult))
            own.wait()
            own.did(dve.tensor_scalar(row_of, row_of, -1.0, None, ALU.add))

            count, more, upto, first, flag, base = (cnt[:, i, :] for i in range(6))
            dve.wait_ge(count_done, TILES + 1)
            own.did(dve.tensor_copy(count, C[0:1, 0:E]))
            own.wait()
            own.did(dve.tensor_reduce(top[:, 0:1], count, AX.X, ALU.max))
            own.did(dve.tensor_copy(keep["fill"][:, 0:E], count))
            own.wait()
            own.did(dve.tensor_scalar(passed_by, limit, top[:, 0:1], None, ALU.is_lt))
            own.wait()
            own.did(dve.tensor_reduce(top[:, 1:2], passed_by, AX.X, ALU.add))
            own.wait()
            dve.tensor_scalar(rounds[:], top[:, 1:2], 1.0, None, ALU.add).then_inc(rounds_known, 1)
            own.clear()
            dve.wait_ge(rounds_known, 1)
            n_rounds = dve.value_load(rounds[0:1, 0:1], min_val=1, max_val=ROUNDS)
            with dve.If(n_rounds > 1):
                own.did(dve.tensor_scalar(more, count, CAP + 0.5, None, ALU.is_gt))
                own.did(dve.memset(one_f[:], 1.0))
                own.wait()
                for r in range(2, ROUNDS):
                    own.did(dve.tensor_scalar(flag, count, r * CAP + 0.5, None, ALU.is_gt))
                    own.wait()
                    own.did(dve.tensor_tensor(more, more, flag, ALU.add))
                    own.wait()
                own.did(dve.tensor_tensor_scan(upto, one_f[:, 0:E], more, 0.0, ALU.mult, ALU.add))
                own.wait()
                own.did(dve.tensor_tensor(first, upto, more, ALU.subtract))
                own.wait()
                own.did(dve.tensor_scalar(first, first, float(CAP), float(OVER_ROW - SPARE_ROW), ALU.mult, ALU.add))
                own.wait()
                for r in range(1, ROUNDS):
                    own.did(dve.tensor_scalar(flag, more, r - 0.5, None, ALU.is_gt))
                    own.did(dve.tensor_scalar(base, first, float((r - 1) * CAP), None, ALU.add))
                    own.wait()
                    own.did(dve.tensor_tensor(base, base, flag, ALU.mult))
                    own.wait()
                    own.did(dve.tensor_scalar(y_row[:, r * E:(r + 1) * E], base, float(SPARE_ROW), None, ALU.add))
                    own.wait()
                own.did(dve.scalar_tensor_tensor(out=base, in0=iota_e[0:1, :], scalar=-float(CAP), in1=first,
                                                 op0=ALU.mult, op1=ALU.add))
                own.wait()
                dve.tensor_scalar(base, base, float(SPARE_ROW - CAP), None, ALU.add).then_inc(shift_ready, 1)
                dve.wait_ge(count_done, TILES + 2)
                own.did(dve.tensor_copy(shift[:], C[:, 0:E]))
                own.wait()
                for t in range(TILES):
                    own.did(dve.tensor_tensor(
                        hot[:], iota_e.rearrange("p (a e) -> p a e", a=1).broadcast_to([P, TOP, E]),
                        idx8[:, t, :].rearrange("p (k e) -> p k e", e=1).broadcast_to([P, TOP, E]), ALU.is_equal))
                    own.wait()
                    hot_sum(shift[:], sel8[:])
                    own.did(dve.tensor_scalar(v8[:], pos8[:, t, :], CAP + 0.5, None, ALU.is_gt))
                    own.wait()
                    own.did(dve.tensor_tensor(sel8[:], sel8[:], v8[:], ALU.mult))
                    own.wait()
                    own.did(dve.tensor_tensor(row_of[:, t * TOP:(t + 1) * TOP], row_of[:, t * TOP:(t + 1) * TOP],
                                              sel8[:], ALU.add))
                own.clear()
            own.did(dve.tensor_tensor(
                tmp[:, 1, :].rearrange("p (t k) -> p t k", k=TOP), row_of.rearrange("p (t k) -> p t k", k=TOP),
                valid[:].rearrange("p (t k) -> p t k", k=1).broadcast_to([P, TILES, TOP]), ALU.mult))
            own.wait()
            own.did(dve.tensor_copy(slots[:], tmp[:, 1, :]))
            own.wait()



def experts(nc, a, c, keep, rows_dram, y_dram):
    ident, place, rounds, y_row = (keep[n] for n in ("ident", "place", "rounds", "y_row"))
    raw = dict(g=keep["raw_g"], u=keep["raw_u"], d=keep["raw_d"])
    ld = dict(g=keep["g_ld"], u=keep["u_ld"], d=keep["d_ld"])
    with ExitStack() as ctx:
        def sb(name, shape, dt=F32):
            return ctx.enter_context(nc.sbuf_tensor(name, shape, dt))

        def sem(name):
            return ctx.enter_context(nc.semaphore(name))

        hi = {m: keep[f"hi_{m}"] for m in "gud"}
        lo = {m: keep[f"lo_{m}"] for m in "gud"}
        x_hi = sb("x_hi", [P, KC, CAP], F32R)
        x_lo = sb("x_lo", [P, KC, CAP], F32R)
        h_hi = sb("h_hi", [P, FC, CAP], F32R)
        h_lo = sb("h_lo", [P, FC, CAP], F32R)
        rows = sb("rows", [P, 2, D])
        y = sb("y", [P, 2, D])
        sig = sb("sig", [P, FC, CAP])
        h1 = sb("h1", [P, FC, CAP])
        h2 = sig
        hot = sb("hot_slots", [P, TILES, 2 * P], BF16)
        iota1, tok = keep["iota1"], keep["tok"]
        idx = sb("idx", [P, 2], I32)
        idx_f = sb("idx_f", [P, 2])
        warm = sb("warm", [1, 2])

        GU = [ctx.enter_context(nc.psum_tensor(f"GU{i}", [P, 512], F32)) for i in range(2)]
        T = [ctx.enter_context(nc.psum_tensor(f"T{i}", [P, 512], F32)) for i in range(4)]
        Y = [ctx.enter_context(nc.psum_tensor(f"Y{i}", [P, 512], F32)) for i in range(2)]
        L = T[3][:, 2 * CAP:2 * CAP + 4]

        lo_set = {m: keep[f"lo_set_{m}"] for m in "gud"}
        hot_ready, l_done, idx_ready, rows_ld, x_tr, x_hi_ev, x_lo_ev = (
            sem(n) for n in ("hot_ready", "l_done", "idx_ready", "rows_ld", "x_tr3", "x_hi_ev", "x_lo_ev"))
        g_used, gu_done, sig_ready, h_ready, y_done, y_ev, y_st = (
            sem(n) for n in ("g_used", "gu_done", "sig_ready", "h_ready3", "y_done3", "y_ev", "y_st"))
        act_passed, warmed, gate_ld, gate_passed = (sem(n) for n in ("act_passed", "warmed", "gate_ld", "gate_passed"))
        gate_w = a["w_ple_gate"][0].rearrange("(p k) n -> p (k n)", k=KC)
        GATE_PIECE = KC * D // E
        dve_own, pool_on = sem("dve_own_experts"), sem("pool_on")
        NJ = E + 1
        NL = E + 2
        NH = E + 3

        block = ctx.enter_context(nc.Block())

        def each_round(eng, body):
            n = eng.value_load(rounds[0:1, 0:1], min_val=1, max_val=ROUNDS)
            with eng.Fori(0, n) as r:
                body(r)

        @block.sync
        def _(sp):
            def load(e, m):
                for name, w in (("g", "w_exp_gate"), ("u", "w_exp_up"), ("d", "w_exp_down")):
                    src = a[w][0][bass.ds(e, 1)]
                    src = (src.rearrange("e (f p) d -> p (e f) d", p=P) if name == "d" else
                           src.rearrange("e (p k) f -> p (e k) f", k=KC))
                    sp.wait_ge(lo_set[name], m + 1)
                    sp.dma_start(raw[name][:], src).then_inc(ld[name], 16)

            sp.dma_start(output_weights(keep)[1], a["w_ple_proj"][0].rearrange("(f p) d -> p f d", p=P)).then_inc(
                y_st, 16)
            ple = keep["ple"]
            for dst, src in ((ple[:, 0:PROMPT_TILES, :], a["p_prompt"][0, 0].rearrange("(t p) d -> p t d", p=P)),
                             (ple[0:NS, SAMPLE, :], a["p_sample"][0].rearrange("b s d -> (b s) d"))):
                sp.dma_start(dst, src).then_inc(keep["output_ld"], 16)

            sp.wait_ge(rows_ld, 32)

            def one_round(r):
                with sp.Fori(0, E - 1) as n:
                    e = sp.snap(n + 1)
                    at = sp.snap(n * GATE_PIECE)
                    load(e, r * E + n)
                    sp.dma_start(keep["w_big"][:, bass.ds(at, GATE_PIECE)], gate_w[:, bass.ds(at, GATE_PIECE)]).then_inc(
                        gate_ld, 16)
                load(0, r * E + (E - 1))
                last = slice((E - 1) * GATE_PIECE, E * GATE_PIECE)
                sp.dma_start(keep["w_big"][:, last], gate_w[:, last]).then_inc(gate_ld, 16)
                sp.wait_ge(gate_ld, 16 * E * r + 16 * E)
                sp.sem_inc(gate_passed, 1)
            each_round(sp, one_round)

        @block.gpsimd
        def _(pool):
            pool.memset(hot[:, :, CAP:2 * P], 0.0).then_inc(pool_on, 1)
            pool.memset(warm[:], 0.0).then_inc(pool_on, 1)

            def one_round(r):
                with pool.Fori(0, NL) as k:
                    pool_after(pool, keep["passed"], idx_ready, r * NL + k + 2)
                    pool_after(pool, keep["passed"], x_tr, 4 * (r * NJ + k) + 1)
                    for b in range(2):
                        pool.indirect_dma_start(
                            out=rows[0:BLK[b], b, :], out_offset=None, in_=rows_dram[:, :],
                            in_offset=bass.IndirectOffsetOnAxis(ap=idx[0:BLK[b], b:b + 1], axis=0),
                        ).then_inc(rows_ld, 16)
                pool_after(pool, keep["passed"], rows_ld, 32 * NL * r + 32 * NL)
            each_round(pool, one_round)

        @block.tensor
        def _(pe):
            def three(out, lhs, rhs, first, last):
                for i, (x, w) in enumerate(((0, 0), (0, 1), (1, 0))):
                    ins = pe.matmul(out, lhs[x], rhs[w], start=first and i == 0, stop=last and i == 2)
                return ins

            def make_list(j, h, rows_read):
                pe.wait_ge(hot_ready, h + 1)
                pe.wait_ge(idx_ready, j + 1)
                pe.wait_ge(x_lo_ev, rows_read)
                for b in range(2):
                    for t in range(TILES):
                        ins = pe.matmul(L[:, 2 * b:2 * b + 2], hot[:, t, b * P:(b + 1) * P], tok[:, t, :],
                                        start=(t == 0), stop=(t == TILES - 1))
                ins.then_inc(l_done, 1)

            def transposes(j, gathered):
                pe.wait_ge(rows_ld, 32 * gathered)
                for i in range(4):
                    bank = T[i]
                    if i == 0:
                        pe.wait_ge(x_lo_ev, 4 * j + 1)
                    for k in range(2):
                        for b in range(2):
                            ins = pe.transpose(bank[:, k * CAP + b * P:k * CAP + b * P + BLK[b]],
                                               rows[0:BLK[b], b, (2 * i + k) * P:(2 * i + k + 1) * P],
                                               ident[0:BLK[b], 0:BLK[b]])
                    ins.then_inc(x_tr, 1)

            def gate_up(m):
                for mat, off in (("g", 0), ("u", CAP)):
                    pe.wait_ge(lo_set[mat], m + 1)
                    for f in range(FC):
                        for k in range(KC):
                            w = slice(f * P, (f + 1) * P)
                            ins = three(GU[f][:, off:off + CAP], (hi[mat][:, k, w], lo[mat][:, k, w]),
                                        (x_hi[:, k, :], x_lo[:, k, :]), k == 0, k == KC - 1)
                        if mat == "u":
                            ins.then_inc(gu_done, 1)
                    if mat == "g":
                        ins.then_inc(g_used, 1)

            def down(m):
                filled = pe.value_load(keep["fill"][0:1, bass.ds(m, 1)], min_val=0, max_val=SEQ + NS)
                pe.wait_ge(lo_set["d"], m + 1)
                with pe.If(filled > P):
                    down_block(m, 0, 1)
                    down_block(m, 1, 1)
                with pe.If(filled < P + 1):
                    down_block(m, 0, 3)

            def down_block(m, b, counts):
                for half in range(2):
                    q = 2 * b + half
                    rows_b = slice(b * P, b * P + BLK[b])
                    cols = slice(half * 512, (half + 1) * 512)
                    pe.wait_ge(y_ev, 4 * m + q + 1)
                    for f in range(FC):
                        if q == 0:
                            pe.wait_ge(h_ready, 2 * m + f + 1)
                        ins = three(Y[half][0:BLK[b], :], (h_hi[:, f, rows_b], h_lo[:, f, rows_b]),
                                    (hi["d"][:, f, cols], lo["d"][:, f, cols]), f == 0, f == FC - 1)
                    ins.then_inc(y_done, counts if half else 1)

            pe.wait_ge(pool_on, 1)

            def one_round(r):
                make_list(r * NL, r * NH, 4 * r * NJ + 1)
                transposes(r * NJ, r * NL + 1)
                make_list(r * NL + 1, r * NH + 1, 4 * r * NJ + 5)
                with pe.Fori(0, E) as n:
                    pe.wait_ge(x_lo_ev, 4 * (r * NJ + n) + 5)
                    gate_up(r * E + n)
                    make_list(r * NL + n + 2, r * NH + n + 2, 4 * (r * NJ + n) + 5)
                    transposes(r * NJ + n + 1, r * NL + n + 2)
                    down(r * E + n)
            each_round(pe, one_round)

        @block.scalar
        def _(act):
            def x_parts(j):
                for i in range(4):
                    act.wait_ge(x_tr, 4 * j + i + 2)
                    act.activation(x_hi[:, 2 * i:2 * i + 2, :], T[i][:, 0:2 * CAP].rearrange(
                        "p (k q) -> p k q", k=2), ACT.Copy).then_inc(x_hi_ev, 1)

            act.sem_inc(x_tr, 1)
            act.sem_inc(y_ev, 1)
            act.wait_ge(pool_on, 2)

            def copy_out(m, q):
                b, half = divmod(q, 2)
                act.wait_ge(y_done, 4 * m + q + 1)
                act.activation(y[0:BLK[b], b, half * 512:(half + 1) * 512], Y[half][0:BLK[b], :],
                               ACT.Copy).then_inc(y_ev, 1)

            def store(first, m, b):
                at = act.snap(first + b * P)
                act.wait_ge(y_ev, 4 * m + 2 * b + 4)
                act.dma_start(y_dram[bass.ds(at, BLK[b])], y[0:BLK[b], b, :]).then_inc(y_st, 16)

            def one_round(r):
                x_parts(r * NJ)
                with act.Fori(0, E) as n:
                    m = r * E + n
                    j = r * NJ + n + 1
                    first = act.value_load(y_row[0:1, bass.ds(m, 1)], min_val=0, max_val=SPARE_ROW)
                    act.activation(warm[:], warm[:], ACT.Sigmoid).then_inc(warmed, 1)
                    act.wait_ge(ld["g"], 16 * m + 32)
                    act.wait_ge(g_used, m + 1)
                    split_hi(act, keep, "g", m + 1, 0)
                    for f in range(FC):
                        act.wait_ge(gu_done, 2 * m + f + 1)
                        act.activation(sig[:, f, :], GU[f][:, 0:CAP], ACT.Sigmoid).then_inc(sig_ready, 1)
                    x_parts(j)
                    act.wait_ge(ld["u"], 16 * m + 32)
                    split_hi(act, keep, "u", m + 1, 0)
                    act.wait_ge(y_st, 32 * m + 16)
                    copy_out(m, 0)
                    split_hi(act, keep, "u", m + 1, 1)
                    copy_out(m, 1)
                    store(first, m, 0)
                    copy_out(m, 2)
                    copy_out(m, 3)
                    store(first, m, 1)
                    act.wait_ge(ld["d"], 16 * m + 32)
                    split_hi(act, keep, "d", m + 1, 0)
                act.wait_ge(y_st, 32 * E * r + 32 * E + 16)
                act.sem_inc(act_passed, 1)
            each_round(act, one_round)

        @block.vector
        def _(dve):
            own = Chain(dve, dve_own)

            def one_hot(j, e):
                dve.wait_ge(l_done, j + 1)
                dve.tensor_tensor(hot[:, :, 0:CAP],
                                  iota1[:].rearrange("p (a s) -> p a s", a=1).broadcast_to([P, TILES, CAP]),
                                  place[:, e, :].rearrange("p (t a) -> p t a", a=1).broadcast_to([P, TILES, CAP])
                                  if isinstance(e, int) else
                                  place[:, bass.ds(e, 1), :].rearrange("p a t -> p t a").broadcast_to(
                                      [P, TILES, CAP]),
                                  ALU.is_equal).then_inc(hot_ready, 1)

            def to_index(j):
                dve.wait_ge(l_done, j + 2)
                own.did(dve.tensor_reduce(idx_f[:], L.rearrange("p (b a) -> p b a", a=2), AX.X, ALU.add))
                own.wait()
                dve.tensor_copy(idx[:], idx_f[:]).then_inc(idx_ready, 1)

            def x_parts(j):
                for i in range(4):
                    w = slice(2 * i, 2 * i + 2)
                    dve.wait_ge(x_hi_ev, 4 * j + i + 1)
                    dve.tensor_tensor(x_lo[:, w, :], T[i][:, 0:2 * CAP].rearrange("p (k q) -> p k q", k=2),
                                      x_hi[:, w, :].bitcast(F32), ALU.subtract).then_inc(x_lo_ev, 1)

            def hidden(m, f):
                dve.wait_ge(sig_ready, 2 * m + f + 1)
                own.did(dve.tensor_tensor(h1[:, f, :], sig[:, f, :], GU[f][:, 0:CAP], ALU.mult))
                own.wait()
                own.did(dve.tensor_tensor(h2[:, f, :], h1[:, f, :], GU[f][:, CAP:2 * CAP], ALU.mult))
                own.wait()
                own.did(dve.tensor_copy(h_hi[:, f, :], h2[:, f, :]))
                own.wait()
                dve.tensor_tensor(h_lo[:, f, :], h2[:, f, :], h_hi[:, f, :].bitcast(F32),
                                  ALU.subtract).then_inc(h_ready, 1)

            dve.sem_inc(l_done, 1)
            dve.sem_inc(idx_ready, 1)
            dve.sem_inc(x_lo_ev, 1)
            dve.sem_inc(y_ev, 1)

            def one_round(r):
                one_hot(r * NL, 0)
                to_index(r * NL)
                one_hot(r * NL + 1, 1)
                x_parts(r * NJ)
                to_index(r * NL + 1)
                one_hot(r * NL + 2, 2)
                own.clear()
                with dve.Fori(0, E) as n:
                    m = r * E + n
                    following = dve.snap(n + 3)
                    split_lo(dve, keep, "g", m + 1)
                    hidden(m, 0)
                    hidden(m, 1)
                    x_parts(r * NJ + n + 1)
                    split_lo(dve, keep, "u", m + 1)
                    to_index(r * NL + n + 2)
                    one_hot(r * NL + n + 3, following)
                    split_lo(dve, keep, "d", m + 1)
                    own.clear()
                dve.wait_ge(hot_ready, NH * r + NH)
                dve.wait_ge(rows_ld, 32 * NL * r + 32 * NL)
                own.did(dve.tensor_scalar(place[:], place[:], -float(CAP), None, ALU.add))
                own.clear()
            each_round(dve, one_round)



def output_weights(keep):
    return (keep["w_big"][:, 0:KC * D].rearrange("p (k n) -> p k n", k=KC),
            keep["w_big"][:, KC * D:KC * D + PLE // P * D].rearrange("p (f n) -> p f n", f=PLE // P))


def output(nc, a, o, keep, y_dram):
    resid, ident, w8, slots = (keep[n] for n in ("resid", "ident", "w8", "slots"))
    LAST = TILES - 1
    with ExitStack() as ctx:
        def sb(name, shape, dt=F32):
            return ctx.enter_context(nc.sbuf_tensor(name, shape, dt))

        def sem(name):
            return ctx.enter_context(nc.semaphore(name))

        w_gate, w_proj = output_weights(keep)
        ple = keep["ple"]
        g_ple = sb("g_ple", [P, D])
        g_fin = sb("g_fin", [P, D])
        yk = sb("yk", [P, TOP, D])
        idx = sb("idx_k", [P, TOP], I32)
        wk = sb("wk", [P, TOP])
        ple_t = sb("ple_t", [P, PLE])
        row = sb("row4", [P, D])
        colT = sb("colT4", [P, KC, P])
        pT = sb("pT", [P, PLE // P, P])
        gate = sb("gate", [P, D])
        inj = sb("inj", [P, D])
        out = sb("out", [P, D])
        junk = sb("junk4", [P, D], BF16)
        st = sb("st4", [P, 8])
        half = sb("half4", [P, 1])

        X = [ctx.enter_context(nc.psum_tensor(f"OX{i}", [P, 512], F32)) for i in range(2)]
        XP = ctx.enter_context(nc.psum_tensor("OXP", [P, 512], F32))
        J = [ctx.enter_context(nc.psum_tensor(f"OJ{i}", [P, 512], F32)) for i in range(2)]
        G = [ctx.enter_context(nc.psum_tensor(f"OG{i}", [P, 512], F32)) for i in range(2)]

        g_ld, zeroed, idx_ready, wk_ready, added, sumsq, row_ready, x_tr, x_ev = (
            sem(n) for n in ("g_ld4", "zeroed4", "idx_ready4", "wk_ready", "added4", "sumsq4", "row_ready4", "x_tr4",
                             "x_ev4"))
        p_ready, p_tr, p_ev, j_done, g_done, g_ready, injected, fin_sq, out_ready, out_st = (
            sem(n) for n in ("p_ready4", "p_tr", "p_ev", "j_done", "g_done4", "g_ready", "injected", "fin_sq",
                             "out_ready", "out_st"))
        y_ld = [sem(f"y_ld{k}") for k in range(TOP)]
        dve_own = sem("dve_own_output")
        pool_own, rstd_ready, fin_ready = sem("pool_own_output"), sem("rstd_ready4"), sem("fin_ready")

        block = ctx.enter_context(nc.Block())

        @block.sync
        def _(sp):
            sp.dma_start(g_ple[:], a["g_ple"][0:1, :].broadcast_to([P, D])).then_inc(out_st, 16)
            sp.dma_start(g_fin[:], a["g_final"].rearrange("(a d) -> a d", a=1).broadcast_to([P, D])).then_inc(g_ld, 16)
            with sp.Fori(0, PROMPT_TILES) as t:
                at = sp.snap(t * P)
                sp.wait_ge(out_ready, t + 1)
                sp.dma_start(o["y_prompt"][0][bass.ds(at, P)], out[:]).then_inc(out_st, 16)
            sp.wait_ge(out_ready, TILES)
            sp.dma_start(o["y_sample"].rearrange("b s d -> (b s) d"), out[0:NS, :]).then_inc(out_st, 16)
            sp.wait_ge(out_st, 16 * TILES + 16)

        @block.gpsimd
        def _(pool):
            pool.memset(ple[NS:P, SAMPLE, :], 0.0).then_inc(zeroed, 1)
            pool.wait_ge(zeroed, 1)
            pool.memset(half[:], -0.5).then_inc(zeroed, 1)
            n_rounds = pool.value_load(keep["rounds"][0:1, 0:1], min_val=1, max_val=ROUNDS)

            def gathers(t):
                pool_after(pool, keep["passed"], added, TOP * t)
                pool.tensor_copy(idx[:], slots[:, bass.ds(t * TOP, TOP)]).then_inc(idx_ready, 1)
                pool.tensor_copy(wk[:], w8[:, t, :]).then_inc(wk_ready, 1)
                pool_after(pool, keep["passed"], idx_ready, t + 1)
                for several, table in ((n_rounds < 2, y_dram[0:OVER_ROW, :]), (n_rounds > 1, y_dram[:, :])):
                    with pool.If(several):
                        for k in range(TOP):
                            pool.indirect_dma_start(
                                out=yk[:, k, :], out_offset=None, in_=table,
                                in_offset=bass.IndirectOffsetOnAxis(ap=idx[:, k:k + 1], axis=0)).then_inc(y_ld[k], 16)

            def ple_inputs(t):
                if isinstance(t, int) and t == 0:
                    pool.wait_ge(keep["output_ld"], 16 * 2)
                else:
                    pool_after(pool, keep["passed"], p_tr, t)
                pool.tensor_copy(ple_t[:], ple[:, t, :]).then_inc(p_ready, 1)

            own = Chain(pool, pool_own)
            pool.wait_ge(zeroed, 2)

            def norm_in(t):
                pool_after(pool, keep["passed"], sumsq, t + 1)
                rstd(own, pool, st[:, 1:2], st[:, 0:1], D, half[:], rstd_ready)

            def norm_out(t):
                pool_after(pool, keep["passed"], fin_sq, t + 1)
                rstd(own, pool, st[:, 5:6], st[:, 4:5], D, half[:], fin_ready)
                own.clear()

            gathers(0)
            ple_inputs(0)
            norm_in(0)
            gathers(1)
            ple_inputs(1)
            own.clear()
            with pool.Fori(0, LAST - 1) as t:
                norm_in(t + 1)
                gathers(t + 2)
                norm_out(t)
                ple_inputs(t + 2)
            norm_in(LAST)
            norm_out(LAST - 1)
            norm_out(LAST)

        @block.tensor
        def _(pe):
            def ple_transposes(t):
                pe.wait_ge(p_ready, t + 1)
                after(pe, p_ev, t)
                for f in range(PLE // P):
                    ins = pe.transpose(XP[:, f * P:(f + 1) * P], ple_t[:, f * P:(f + 1) * P], ident[:])
                ins.then_inc(p_tr, 1)

            def transposes(t):
                pe.wait_ge(row_ready, t + 1)
                after(pe, x_ev, 2 * t)
                for b in range(2):
                    for k in range(4):
                        ins = pe.transpose(X[b][:, k * P:(k + 1) * P], row[:, (4 * b + k) * P:(4 * b + k + 1) * P],
                                           ident[:])
                    ins.then_inc(x_tr, 1)

            def tile(t, last=False):
                pe.wait_ge(x_ev, 2 * t + 2)
                after(pe, g_ready, 2 * t)
                for half in range(2):
                    for k in range(KC):
                        ins = pe.matmul(G[half][:], colT[:, k, :], w_gate[:, k, half * 512:(half + 1) * 512],
                                        start=(k == 0), stop=(k == KC - 1))
                    ins.then_inc(g_done, 1)
                if not last:
                    transposes(t + 1)
                pe.wait_ge(p_ev, t + 1)
                after(pe, injected, 2 * t)
                for half in range(2):
                    for f in range(PLE // P):
                        ins = pe.matmul(J[half][:], pT[:, f, :], w_proj[:, f, half * 512:(half + 1) * 512],
                                        start=(f == 0), stop=(f == PLE // P - 1))
                    ins.then_inc(j_done, 1)
                if not last:
                    ple_transposes(t + 1)

            ple_transposes(0)
            transposes(0)
            pe.wait_ge(keep["output_ld"], 16 * 2)
            tile(0)
            with pe.Fori(1, LAST) as t:
                tile(t)
            tile(LAST, last=True)

        @block.scalar
        def _(act):
            def square_sum(t):
                act.wait_ge(added, TOP * t + TOP)
                after(act, fin_sq, t - 1)
                act.activation(junk[:], resid[:, t, :], ACT.Square, accum_out=st[:, 0:1]).then_inc(sumsq, 1)

            def p_copy(t):
                act.wait_ge(p_tr, t + 1)
                act.activation(pT[:].rearrange("p f q -> p (f q)"), XP[:, 0:PLE], ACT.Copy).then_inc(p_ev, 1)

            def col_copy(t):
                act.wait_ge(x_tr, 2 * t + 1)
                act.activation(colT[:, 0:4, :], X[0][:].rearrange("p (k q) -> p k q", k=4),
                               ACT.Copy).then_inc(x_ev, 1)

            def tile(t, last=False):
                if not last:
                    square_sum(t + 1)
                for half in range(2):
                    act.wait_ge(g_done, 2 * t + half + 1)
                    act.activation(gate[:, half * 512:(half + 1) * 512], G[half][:], ACT.Sigmoid).then_inc(g_ready, 1)
                if not last:
                    col_copy(t + 1)
                    p_copy(t + 1)
                act.wait_ge(injected, 2 * t + 2)
                act.activation(junk[:], resid[:, t, :], ACT.Square, accum_out=st[:, 4:5]).then_inc(fin_sq, 1)

            square_sum(0)
            p_copy(0)
            col_copy(0)
            tile(0)
            with act.Fori(1, LAST) as t:
                tile(t)
            tile(LAST, last=True)

        @block.vector
        def _(dve):
            own = Chain(dve, dve_own)

            def gather_sum(t, ks):
                if ks[0] == 0:
                    dve.wait_ge(wk_ready, t + 1)
                for k in ks:
                    dve.wait_ge(y_ld[k], 16 * (t + 1))
                    if k:
                        dve.wait_ge(added, TOP * t + k)
                    dve.scalar_tensor_tensor(out=resid[:, t, :], in0=yk[:, k, :], scalar=wk[:, k:k + 1],
                                             in1=resid[:, t, :], op0=ALU.mult, op1=ALU.add).then_inc(added, 1)

            def norm(t):
                dve.wait_ge(rstd_ready, t + 1)
                dve.scalar_tensor_tensor(out=row[:].rearrange("p (k q) -> p q k", k=KC),
                                         in0=resid[:, t, :].rearrange("p (q k) -> p q k", k=KC), scalar=st[:, 1:2],
                                         in1=g_ple[:].rearrange("p (q k) -> p q k", k=KC),
                                         op0=ALU.mult, op1=ALU.mult).then_inc(row_ready, 1)

            def col_copy(t):
                dve.wait_ge(x_tr, 2 * t + 2)
                dve.tensor_copy(colT[:, 4:8, :], X[1][:].rearrange("p (k q) -> p k q", k=4)).then_inc(x_ev, 1)

            def inject(t, ahead=lambda k: None):
                for half in range(2):
                    ahead(half)
                    w = slice(half * 512, (half + 1) * 512)
                    dve.wait_ge(g_ready, 2 * t + half + 1)
                    dve.wait_ge(j_done, 2 * t + half + 1)
                    own.did(dve.tensor_tensor(inj[:, w], gate[:, w], J[half][:], ALU.mult))
                    own.wait()
                    dve.tensor_tensor(resid[:, t, w], resid[:, t, w], inj[:, w], ALU.add).then_inc(injected, 1)

            def finish(t):
                dve.wait_ge(fin_ready, t + 1)
                dve.wait_ge(out_st, 16 * t + 16)
                dve.scalar_tensor_tensor(out=out[:], in0=resid[:, t, :], scalar=st[:, 5:6], in1=g_fin[:],
                                         op0=ALU.mult, op1=ALU.mult).then_inc(out_ready, 1)

            def following(t, first, between):
                gather_sum(t, range(first, TOP))
                between()
                norm(t)
                col_copy(t)

            dve.wait_ge(out_st, 16)
            following(0, 0, lambda: dve.wait_ge(g_ld, 16))
            following(1, 0, lambda: None)
            inject(0, lambda k: gather_sum(2, (k,)))
            own.clear()
            with dve.Fori(1, LAST - 1) as t:
                following(t + 1, 2, lambda: finish(t - 1))
                inject(t, lambda k: gather_sum(t + 2, (k,)))
                own.clear()
            following(LAST, 2, lambda: finish(LAST - 2))
            inject(LAST - 1)
            finish(LAST - 1)
            inject(LAST)
            finish(LAST)



def constants():
    c = {}
    f = np.float32
    inv = np.power(f(THETA), -np.arange(HALF, dtype=f) * f(2.0) / f(2 * HALF)).astype(f)
    pos = np.zeros((TILES, P), f)
    pos[:PROMPT_TILES] = np.arange(SEQ).reshape(PROMPT_TILES, P)
    pos[SAMPLE, :NS] = PAST + np.arange(NS) % STEPS
    ang = (pos[:, :, None] * inv[None, None, :]).astype(f)
    c["rope"] = np.stack([np.cos(ang), np.sin(ang)], axis=2).transpose(1, 0, 2, 3).astype(f)
    q, k = np.arange(P)[:, None], np.arange(2 * P)[None, :]
    later = (k >= q) & (k <= q + P)
    c["amask"] = np.where(np.stack([later & (k >= P), later], axis=1), f(0), f(NEG)).astype(f)
    rows = np.arange(P)
    i, s = rows // 32, rows % STEPS
    sm = np.full((P, 2, P + NS), NEG, f)
    for h in range(2):
        sm[:, h, :P][np.arange(P)[None, :] >= s[:, None]] = 0
        kb, ks = np.arange(NS) // STEPS, np.arange(NS) % STEPS
        sm[:, h, P:][(kb[None, :] == (4 * h + i)[:, None]) & (ks[None, :] <= s[:, None])] = 0
    c["smask"] = sm
    pick = np.zeros((P, KV_HEADS, HEADS), f)
    for g in range(KV_HEADS):
        pick[rows, g, GROUP * g + (rows % 32) // STEPS] = 1
    c["pick"] = pick
    pm = np.zeros((P, 3, PG, P), f)
    src, dst = np.arange(P)[:, None], np.arange(P)[None, :]
    for g, w in enumerate(POOL_WINDOWS):
        inside = (src <= dst) & (src > dst - w)
        pm[:, 0, g] = inside / np.minimum(dst + 1, w) - (src == dst)
        pm[:, 1, g] = inside / w - (src == dst)
        pm[:, 2, g] = (src - P > dst - w) / w
    c["pmat"] = pm.astype(f)
    ps = np.zeros((P, 2, PG, NS), f)
    db, ds_ = np.arange(NS) // STEPS, np.arange(NS) % STEPS
    nb, nstep = np.arange(NS) // STEPS, np.arange(NS) % STEPS
    sb_, sr = np.arange(SEQS * PREFIX) // PREFIX, np.arange(SEQS * PREFIX) % PREFIX - PREFIX
    for g, w in enumerate(POOL_WINDOWS):
        same = nb[:, None] == db[None, :]
        ps[:NS, 0, g] = (same & (nstep[:, None] <= ds_) & (nstep[:, None] > ds_ - w)) / w - np.eye(NS)
        ps[:SEQS * PREFIX, 1, g] = ((sb_[:, None] == db[None, :]) & (sr[:, None] > ds_ - w)) / w
    c["pmat_s"] = ps.astype(f)
    c["tri"] = (src < dst).astype(f)
    c["iota_e"] = np.broadcast_to(np.arange(E, dtype=f), (P, E)).copy()
    v = np.ones((P, TILES), f)
    v[NS:, SAMPLE] = 0
    c["valid"] = v
    c["iota1"] = np.broadcast_to(np.arange(1, CAP + 1), (P, CAP)).astype(f)
    tok = np.zeros((P, TILES, 2))
    tok[:, :, 0] = np.arange(P)[:, None]
    tok[:, :, 1] = P * np.arange(TILES)[None, :]
    c["tok"] = tok.astype(f)
    return c


OUTS = {
    "y_prompt": (1, SEQ, D), "y_sample": (SEQS, STEPS, D),
    "k_prompt": (1, 1, WINDOW, KV_HEADS, HD), "v_prompt": (1, 1, WINDOW, KV_HEADS, HD),
    "pool_prompt": (1, 1, PREFIX, POOL),
    "k_sample": (1, SEQS, WINDOW, KV_HEADS, HD), "v_sample": (1, SEQS, WINDOW, KV_HEADS, HD),
    "pool_sample": (1, SEQS, PREFIX, POOL),
}


def kernel(**inputs):
    import concourse.bacc as bacc
    from concourse.bass_utils import run_bass_kernel_spmd as run

    nc = bacc.Bacc("TRN2", target_bir_lowering=False, num_devices=1)
    arrays = {}

    def declare(prefix, named):
        aps = {}
        for name, x in named.items():
            x = np.ascontiguousarray(x)
            arrays[f"{prefix}_{name}"] = x
            aps[name] = nc.dram_tensor(f"{prefix}_{name}", x.shape, mybir.dt.from_np(x.dtype),
                                       kind="ExternalInput").ap()
        return aps

    a = declare("in", inputs)
    c = declare("const", constants())
    o = {name: nc.dram_tensor(f"out_{name}", shape, F32, kind="ExternalOutput").ap() for name, shape in OUTS.items()}
    build(nc, a, o, c)
    r = run(nc, [arrays], core_ids=[0]).results[0]
    return tuple(r[f"out_{name}"] for name in OUTS)
```
